# Optimizing a Trainium2 kernel written in Bass

```python
import jax, jax.numpy as jnp
from jax import lax
import numpy as np
import math

D_MODEL = 1024
BATCH = 1
SEQ = 256
DEPTH = 1

HEAD_DIM = 64
N_HEADS = D_MODEL // HEAD_DIM
N_FOX_HEADS = N_HEADS // 2
N_SB_HEADS = N_HEADS - N_FOX_HEADS
FOX_WIDTH = N_FOX_HEADS * HEAD_DIM
SB_WIDTH = N_SB_HEADS * HEAD_DIM
MIX_WIDTH = FOX_WIDTH + SB_WIDTH
IN_COLS = 3 * FOX_WIDTH + N_FOX_HEADS + 3 * SB_WIDTH
D_FF = ((8 * D_MODEL // 3 + 127) // 128) * 128
CONV_WIDTH = 3
BLOCK_Q = 128
EPS = 1e-6


def rmsnorm(x, g):
    xf = x.astype(jnp.float32)
    y = xf * lax.rsqrt(jnp.mean(xf * xf, axis=-1, keepdims=True) + EPS)
    return (y * g.astype(jnp.float32)).astype(x.dtype)

def split_heads(t, n_heads):
    b, s, _ = t.shape
    return t.reshape(b, s, n_heads, HEAD_DIM).transpose(0, 2, 1, 3)

def merge_heads(t):
    b, h, s, d = t.shape
    return t.transpose(0, 2, 1, 3).reshape(b, s, h * d)

def to_blocks(t):
    b, h, s = t.shape[:3]
    t = t.reshape(b, h, s // BLOCK_Q, BLOCK_Q, *t.shape[3:])
    return jnp.moveaxis(t, 2, 0)

def from_blocks(t):
    nb, b, h, bq, d = t.shape
    return jnp.moveaxis(t, 0, 2).reshape(b, h, nb * bq, d)

def fox_attention(q, k, v, log_f):
    s_len = q.shape[2]
    scale = HEAD_DIM ** -0.5
    kf = k.astype(jnp.float32)
    vf = v.astype(jnp.float32)
    F = jnp.cumsum(log_f, axis=-1)
    kpos = jnp.arange(s_len)

    def block(args):
        i, qi, Fi = args
        qpos = i * BLOCK_Q + jnp.arange(BLOCK_Q)
        logits = (jnp.einsum('bhqd,bhkd->bhqk', qi.astype(jnp.float32), kf) * scale
                  + Fi[..., :, None] - F[:, :, None, :])
        logits = jnp.where(kpos[None, :] <= qpos[:, None], logits, -jnp.inf)
        p = jax.nn.softmax(logits, axis=-1)
        return jnp.einsum('bhqk,bhkd->bhqd', p, vf)

    out = lax.map(block, (jnp.arange(s_len // BLOCK_Q), to_blocks(q), to_blocks(F)))
    return from_blocks(out).astype(v.dtype)

def stick_breaking_attention(q, k, v):
    s_len = q.shape[2]
    scale = HEAD_DIM ** -0.5
    kf = k.astype(jnp.float32)
    vf = v.astype(jnp.float32)
    kpos = jnp.arange(s_len)

    def block(args):
        i, qi = args
        qpos = i * BLOCK_Q + jnp.arange(BLOCK_Q)
        mask = kpos[None, :] < qpos[:, None]
        z = jnp.einsum('bhqd,bhkd->bhqk', qi.astype(jnp.float32), kf) * scale
        log_beta = jax.nn.log_sigmoid(z)
        log_one_minus = jnp.where(mask, jax.nn.log_sigmoid(-z), 0.0)
        after = lax.cumsum(log_one_minus, axis=3, reverse=True) - log_one_minus
        weights = jnp.where(mask, jnp.exp(log_beta + after), 0.0)
        return jnp.einsum('bhqk,bhkd->bhqd', weights, vf)

    out = lax.map(block, (jnp.arange(s_len // BLOCK_Q), to_blocks(q)))
    return from_blocks(out).astype(v.dtype)

def causal_dwconv(u, w, b):
    s_len = u.shape[1]
    up = jnp.pad(u, ((0, 0), (CONV_WIDTH - 1, 0), (0, 0)))
    out = b + w[0] * up[:, 0:s_len]
    for kk in range(1, CONV_WIDTH):
        out = out + w[kk] * up[:, kk:kk + s_len]
    return out

def first_inputs(seed: int = 0) -> dict:
    key = jax.random.key(seed)
    ks = jax.random.split(key, 13)
    f32 = jnp.float32
    x = jax.random.normal(ks[0], (BATCH, SEQ, D_MODEL), f32)
    attn_norm_g = 1.0 + 0.05 * jax.random.normal(ks[1], (DEPTH, D_MODEL), f32)
    w_in = jax.random.normal(ks[2], (DEPTH, D_MODEL, IN_COLS), f32) * D_MODEL ** -0.5
    forget_bias = (jnp.linspace(1.0, 6.0, N_FOX_HEADS, dtype=f32)[None, :]
                   + 0.1 * jax.random.normal(ks[3], (DEPTH, N_FOX_HEADS), f32))
    fox_out_g = 1.0 + 0.05 * jax.random.normal(ks[4], (DEPTH, FOX_WIDTH), f32)
    sb_out_g = 1.0 + 0.05 * jax.random.normal(ks[5], (DEPTH, SB_WIDTH), f32)
    w_out = jax.random.normal(ks[6], (DEPTH, MIX_WIDTH, D_MODEL), f32) * MIX_WIDTH ** -0.5
    ffn_norm_g = 1.0 + 0.05 * jax.random.normal(ks[7], (DEPTH, D_MODEL), f32)
    w_up = jax.random.normal(ks[8], (DEPTH, D_MODEL, 2 * D_FF), f32) * D_MODEL ** -0.5
    conv_w = jax.random.normal(ks[9], (DEPTH, CONV_WIDTH, 2 * D_FF), f32) * CONV_WIDTH ** -0.5
    conv_b = 0.02 * jax.random.normal(ks[10], (DEPTH, 2 * D_FF), f32)
    w_down = jax.random.normal(ks[11], (DEPTH, D_FF, D_MODEL), f32) * D_FF ** -0.5
    final_norm_g = 1.0 + 0.05 * jax.random.normal(ks[12], (D_MODEL,), f32)
    return {"x": x, "attn_norm_g": attn_norm_g, "w_in": w_in, "forget_bias": forget_bias,
            "fox_out_g": fox_out_g, "sb_out_g": sb_out_g, "w_out": w_out,
            "ffn_norm_g": ffn_norm_g, "w_up": w_up, "conv_w": conv_w, "conv_b": conv_b,
            "w_down": w_down, "final_norm_g": final_norm_g}

def first_block(x, attn_norm_g, w_in, forget_bias, fox_out_g, sb_out_g, w_out,
              ffn_norm_g, w_up, conv_w, conv_b, w_down, final_norm_g):
    b, s_len, _ = x.shape
    splits = [FOX_WIDTH, 2 * FOX_WIDTH, 3 * FOX_WIDTH, 3 * FOX_WIDTH + N_FOX_HEADS,
              3 * FOX_WIDTH + N_FOX_HEADS + SB_WIDTH,
              3 * FOX_WIDTH + N_FOX_HEADS + 2 * SB_WIDTH]
    for l in range(DEPTH):
        h = rmsnorm(x, attn_norm_g[l])
        proj = h @ w_in[l]
        fq, fk, fv, f_logit, sq, sk, sv = jnp.split(proj, splits, axis=-1)
        log_f = jax.nn.log_sigmoid(
            (f_logit + forget_bias[l]).astype(jnp.float32)).transpose(0, 2, 1)
        o_fox = fox_attention(split_heads(fq, N_FOX_HEADS), split_heads(fk, N_FOX_HEADS),
                              split_heads(fv, N_FOX_HEADS), log_f)
        o_sb = stick_breaking_attention(split_heads(sq, N_SB_HEADS), split_heads(sk, N_SB_HEADS),
                                        split_heads(sv, N_SB_HEADS))
        o = jnp.concatenate([rmsnorm(merge_heads(o_fox), fox_out_g[l]),
                             rmsnorm(merge_heads(o_sb), sb_out_g[l])], axis=-1)
        x = x + o @ w_out[l]
        h = rmsnorm(x, ffn_norm_g[l])
        u = causal_dwconv(h @ w_up[l], conv_w[l], conv_b[l])
        gate, val = jnp.split(u, 2, axis=-1)
        x = x + (jax.nn.silu(gate) * val) @ w_down[l]
    return rmsnorm(x, final_norm_g)


DEPTH_2 = 2

N_MIXERS = 2
N_HEADS_2 = 8
HEAD_DIM_2 = D_MODEL // N_HEADS_2
ATTN_WIDTH = N_HEADS_2 * HEAD_DIM_2
BLOCK = 256
TOPK_BLOCKS = 3
QUERY_CHUNK = 32
D_FF_2 = int(math.ceil((8 * D_MODEL / 3) / 256) * 256)
N_ATTN_LAYERS = (DEPTH_2 + 1) // 2
N_CONV_LAYERS = DEPTH_2 // 2


def rms_norm(x, gain):
    xf = x.astype(jnp.float32)
    y = xf * lax.rsqrt(jnp.mean(xf * xf, axis=-1, keepdims=True) + EPS)
    return (y * gain.astype(jnp.float32)).astype(x.dtype)

def modulate(x, gain, shift, scale):
    return rms_norm(x, gain) * (1 + scale[:, None, :]) + shift[:, None, :]

def moba_attention(h, w_qkv, w_o, q_gain, k_gain):
    B, S, _ = h.shape
    qkv = (h @ w_qkv).reshape(B, S, 3, N_HEADS_2, HEAD_DIM_2).transpose(2, 0, 3, 1, 4)
    q = rms_norm(qkv[0], q_gain) * (HEAD_DIM_2 ** -0.5)
    k = rms_norm(qkv[1], k_gain)
    v = qkv[2]
    n_blocks = -(-S // BLOCK)
    pad = n_blocks * BLOCK - S
    kp = jnp.pad(k, ((0, 0), (0, 0), (0, pad), (0, 0)))
    vp = jnp.pad(v, ((0, 0), (0, 0), (0, pad), (0, 0)))
    k_blocks = kp.reshape(B, N_HEADS_2, n_blocks, BLOCK, HEAD_DIM_2)
    v_blocks = vp.reshape(B, N_HEADS_2, n_blocks, BLOCK, HEAD_DIM_2)
    k_mean = jnp.mean(k_blocks.astype(jnp.float32), axis=3).astype(k.dtype)
    n_sel = min(TOPK_BLOCKS, n_blocks)
    bi = jnp.arange(B)[:, None, None, None]
    hi = jnp.arange(N_HEADS_2)[None, :, None, None]
    blk_ids = jnp.arange(n_blocks)

    def chunk(ci):
        q0 = ci * QUERY_CHUNK
        nb = q0 // BLOCK
        qc = lax.dynamic_slice_in_dim(q, q0, QUERY_CHUNK, axis=2)
        k_own = lax.dynamic_slice_in_dim(kp, nb * BLOCK, BLOCK, axis=2)
        v_own = lax.dynamic_slice_in_dim(vp, nb * BLOCK, BLOCK, axis=2)
        route = jnp.einsum('bhqd,bhnd->bhqn', qc, k_mean).astype(jnp.float32)
        route = jnp.where(blk_ids < nb, route, -jnp.inf)
        _, idx = lax.top_k(route, n_sel)
        k_sel = k_blocks[bi, hi, idx]
        v_sel = v_blocks[bi, hi, idx]
        qpos = q0 + jnp.arange(QUERY_CHUNK)
        kpos = nb * BLOCK + jnp.arange(BLOCK)
        s_own = jnp.einsum('bhqd,bhkd->bhqk', qc, k_own).astype(jnp.float32)
        s_own = jnp.where(kpos[None, :] <= qpos[:, None], s_own, -jnp.inf)
        s_sel = jnp.einsum('bhqd,bhqjkd->bhqjk', qc, k_sel).astype(jnp.float32)
        slot_ok = jnp.arange(n_sel) < nb
        s_sel = jnp.where(slot_ok[:, None], s_sel, -jnp.inf)
        s_sel = s_sel.reshape(B, N_HEADS_2, QUERY_CHUNK, n_sel * BLOCK)
        p = jax.nn.softmax(jnp.concatenate([s_own, s_sel], axis=-1), axis=-1).astype(v.dtype)
        p_own = p[..., :BLOCK]
        p_sel = p[..., BLOCK:].reshape(B, N_HEADS_2, QUERY_CHUNK, n_sel, BLOCK)
        return (jnp.einsum('bhqk,bhkd->bhqd', p_own, v_own)
                + jnp.einsum('bhqjk,bhqjkd->bhqd', p_sel, v_sel))

    o = lax.map(chunk, jnp.arange(S // QUERY_CHUNK))
    o = o.transpose(1, 0, 3, 2, 4).reshape(B, S, ATTN_WIDTH)
    return o @ w_o

def short_conv(h, w_in, conv_w, w_out):
    S = h.shape[1]
    b_gate, c_gate, u = jnp.split(h @ w_in, 3, axis=-1)
    u = c_gate * u
    up = jnp.pad(u, ((0, 0), (CONV_WIDTH - 1, 0), (0, 0)))
    y = sum(conv_w[j] * up[:, j:j + S] for j in range(CONV_WIDTH))
    return (b_gate * y) @ w_out

def swiglu(h, w_gate_up, w_down):
    g, u = jnp.split(h @ w_gate_up, 2, axis=-1)
    return (jax.nn.silu(g) * u) @ w_down

def second_inputs(seed: int = 0) -> dict:
    key = jax.random.key(seed)
    ks = jax.random.split(key, 16)
    f32 = jnp.float32
    nrm = lambda k, shape, s: (jax.random.normal(k, shape, f32) * s)
    return {
        "x": nrm(ks[0], (BATCH, SEQ, D_MODEL), 1.0),
        "c": nrm(ks[1], (BATCH, D_MODEL), 1.0),
        "w_ada": nrm(ks[2], (DEPTH_2, D_MODEL, 6 * D_MODEL), 0.5 * D_MODEL ** -0.5),
        "b_ada": nrm(ks[3], (DEPTH_2, 6 * D_MODEL), 0.02),
        "norm_mix": 1.0 + nrm(ks[4], (DEPTH_2, D_MODEL), 0.02),
        "norm_ffn": 1.0 + nrm(ks[5], (DEPTH_2, D_MODEL), 0.02),
        "w_qkv": nrm(ks[6], (N_ATTN_LAYERS, D_MODEL, 3 * ATTN_WIDTH), D_MODEL ** -0.5),
        "w_o": nrm(ks[7], (N_ATTN_LAYERS, ATTN_WIDTH, D_MODEL), ATTN_WIDTH ** -0.5),
        "q_gain": 1.0 + nrm(ks[8], (N_ATTN_LAYERS, HEAD_DIM_2), 0.02),
        "k_gain": 1.0 + nrm(ks[9], (N_ATTN_LAYERS, HEAD_DIM_2), 0.02),
        "w_in": nrm(ks[10], (N_CONV_LAYERS, D_MODEL, 3 * D_MODEL), D_MODEL ** -0.5),
        "conv_w": nrm(ks[11], (N_CONV_LAYERS, CONV_WIDTH, D_MODEL), CONV_WIDTH ** -0.5),
        "w_out": nrm(ks[12], (N_CONV_LAYERS, D_MODEL, D_MODEL), D_MODEL ** -0.5),
        "w_gate_up": nrm(ks[13], (DEPTH_2, D_MODEL, 2 * D_FF_2), D_MODEL ** -0.5),
        "w_down": nrm(ks[14], (DEPTH_2, D_FF_2, D_MODEL), D_FF_2 ** -0.5),
    }

def second_block(x, c, w_ada, b_ada, norm_mix, norm_ffn, w_qkv, w_o, q_gain, k_gain,
              w_in, conv_w, w_out, w_gate_up, w_down):
    sc = jax.nn.silu(c)
    for i in range(DEPTH_2):
        mod = sc @ w_ada[i] + b_ada[i]
        sh_m, sc_m, g_m, sh_f, sc_f, g_f = jnp.split(mod, 6, axis=-1)
        h = modulate(x, norm_mix[i], sh_m, sc_m)
        j = i // N_MIXERS
        if i % N_MIXERS == 0:
            y = moba_attention(h, w_qkv[j], w_o[j], q_gain[j], k_gain[j])
        else:
            y = short_conv(h, w_in[j], conv_w[j], w_out[j])
        x = x + g_m[:, None, :] * y
        h = modulate(x, norm_ffn[i], sh_f, sc_f)
        x = x + g_f[:, None, :] * swiglu(h, w_gate_up[i], w_down[i])
    return x


def setup_inputs(seed=0):
    out = dict(first_inputs(seed))
    for name, value in second_inputs(seed + 1).items():
        if name != "x":
            out[name + "_2"] = value
    return out


def reference(
    x, attn_norm_g, w_in, forget_bias, fox_out_g, sb_out_g, w_out, ffn_norm_g, w_up, conv_w,
    conv_b, w_down, final_norm_g, c_2, w_ada_2, b_ada_2, norm_mix_2, norm_ffn_2, w_qkv_2, w_o_2,
    q_gain_2, k_gain_2, w_in_2, conv_w_2, w_out_2, w_gate_up_2, w_down_2,
):
    x = first_block(
        x, attn_norm_g, w_in, forget_bias, fox_out_g, sb_out_g, w_out, ffn_norm_g, w_up, conv_w,
        conv_b, w_down, final_norm_g,
    )
    return second_block(
        x, c_2, w_ada_2, b_ada_2, norm_mix_2, norm_ffn_2, w_qkv_2, w_o_2, q_gain_2, k_gain_2,
        w_in_2, conv_w_2, w_out_2, w_gate_up_2, w_down_2,
    )


_drawn_inputs = setup_inputs


def setup_inputs(seed=0):
    import zlib

    import numpy as np

    out = dict(_drawn_inputs(seed))
    spreads = {}
    factors = {'conv_b': 4.444, 'norm_mix_2': 4.657, 'norm_ffn_2': 6.76, 'q_gain_2': 8.0, 'k_gain_2': 8.0}
    for name, (base, spread) in spreads.items():
        noise = np.random.default_rng([zlib.crc32(name.encode()), seed]).standard_normal(out[name].shape)
        drawn = base * np.exp(spread * noise) if base else spread * noise
        out[name] = __import__('jax').numpy.asarray(drawn.astype(out[name].dtype))
    for name, factor in factors.items():
        out[name] = (out[name] * factor).astype(out[name].dtype)
    return out
```

```python
from contextlib import ExitStack

import concourse.bass as bass
from concourse import mybir

F32 = mybir.dt.float32
F32R = mybir.dt.float32r
ACT = mybir.ActivationFunctionType
ALU = mybir.AluOpType
AX = mybir.AxisListType

P = 128
T = 256
D = 1024
KT = D // P
FF = 2816
FT = FF // P
CW = 256
UNIT = 4 * CW
EPS = 1e-6
NEG = -1e30

IN1, OUT1, UP1, DOWN1 = 0, 12, 16, 38
QKV, OUT2, UP2, DOWN2 = 49, 61, 65, 87
IN3, OUT3, UP3, DOWN3, CHUNKS = 98, 110, 114, 136, 147
RAW = 4
SPLIT = 4
PAIRS = FF // CW
ADA = 24
ADA_W = 2048

V_ATTN, V_FOX, V_SB, V_FFN, V_FINAL, V_MIX2, V_FFN2 = 0, 8, 12, 16, 24, 32, 48
V_QG, V_KG, V_CONV2, V_C, V_ROWS0 = 64, 65, 66, 90, 98
V_TAP = {0: (1, 0), 1: (1, 44), 2: (2, 0)}
V_CONVB = (2, 44)
V_BANKS, X_BANKS = (4, 5, 6, 2), (0, 1, 3, 7)
ROWS = (V_ROWS0, 88, 88, 96)
SH_M, SC_M, G_M, SH_F, SC_F, G_F = (KT * n for n in range(6))


def at(const, step, i):
    return const if i is None else i * step + const


def proj(c):
    return c if c < UP1 else c - QKV + 16 if c < UP2 else c - IN3 + 32


def cols(const, step, i, size):
    return slice(const, const + size) if i is None else bass.ds(i * step + const, size)


def model_kernel(nc, x, attn_norm_g, w_in, forget_bias, fox_out_g, sb_out_g, w_out, ffn_norm_g, w_up,
                 conv_w, conv_b, w_down, final_norm_g, c_2, w_ada_2, b_ada_2, norm_mix_2, norm_ffn_2,
                 w_qkv_2, w_o_2, q_gain_2, k_gain_2, w_in_2, conv_w_2, w_out_2, w_gate_up_2, w_down_2, out):
    ctx = ExitStack()
    with ctx:
        def sb(name, shape, dt=F32, stack=ctx):
            return stack.enter_context(nc.sbuf_tensor(name, shape, dt))

        def sem(name):
            return ctx.enter_context(nc.semaphore(name))

        w_raw = sb("w_raw", [P, RAW, 2 * UNIT])
        w_hi = sb("w_hi", [P, SPLIT, UNIT], F32R)
        w_lo = sb("w_lo", [P, SPLIT, UNIT], F32R)
        res = sb("res", [P, KT, T])
        act_hi = sb("act_hi", [P, KT, T], F32R)
        act_lo = sb("act_lo", [P, KT, T], F32R)
        ada_raw = sb("ada_raw", [P, 2, ADA_W])
        ada_acc = sb("ada_acc", [P, 3, ADA_W])
        vec = sb("vec", [P, 4, P])
        mod = sb("mod", [P, 2, 6 * KT])
        gain2 = sb("gain2", [P, 4, KT])
        silu_c = sb("silu_c", [P, KT])
        qk_gain = sb("qk_gain", [P, 2])
        ident = sb("ident", [P, P])
        ones = sb("ones", [P, P])
        upto = sb("upto", [P, T])
        causal = sb("causal", [P, T])
        later = sb("later", [P, P])
        minus = sb("minus", [P, P])
        before = sb("before", [P, 3 * P])
        rowsum = sb("rowsum", [P, 16, 2])
        nmax = sb("nmax", [P, 16, 2])
        rinv = sb("rinv", [P, 16, 2])
        small = sb("small", [P, 8, 8])
        wf_raw = sb("wf_raw", [P, KT, 8])
        wf_hi = sb("wf_hi", [P, KT, 8], F32R)
        wf_lo = sb("wf_lo", [P, KT, 8], F32R)
        fbias = sb("fbias", [P, 8])
        f_abs = sb("f_abs", [P, 2, 8])
        f_log = sb("f_log", [P, 2, 8])
        f_neg = sb("f_neg", [P, 2, 8])
        nlf = sb("nlf", [P, 2, 8])
        f_cum = sb("f_cum", [P, 2, 8])

        phase = ExitStack()
        scr = sb("scr", [P, KT, T], stack=phase)
        n_a = sb("n_a", [P, T], stack=phase)
        n_y = sb("n_y", [P, T], stack=phase)
        n_t = sb("n_t", [P, T], stack=phase)
        rstd = sb("rstd", [P, T], stack=phase)
        x_in = sb("x_in", [P, 2, D], stack=phase)
        v_in = sb("v_in", [P, 4, P], stack=phase)
        o_sb = sb("o_sb", [P, 2, D], stack=phase)
        phase.close()
        phase = ExitStack()
        q_pad = sb("q_pad", [P, 8, T], stack=phase)
        k_fox = sb("k_fox", [P, 4, T], stack=phase)
        k_pad = sb("k_pad", [P, 8, T], stack=phase)
        q_sb = sb("q_sb", [P, 4, T], stack=phase)
        v_tok = sb("v_tok", [P, 2, D], stack=phase)
        o_tok = sb("o_tok", [P, 2, D], stack=phase)
        logit = sb("logit", [P, 2, 3 * P], stack=phase)
        prob = sb("prob", [P, 2, 3 * P], stack=phase)
        prob_t = sb("prob_t", [P, 2, 3 * P], stack=phase)
        sb_l = sb("sb_l", [P, 2, 3 * P], stack=phase)
        sb_t = sb("sb_t", [P, 3 * P], stack=phase)
        sb_m = sb("sb_m", [P, 2, 3 * P], stack=phase)
        sb_b = sb("sb_b", [P, 2, 3 * P], stack=phase)
        phase.close()
        phase = ExitStack()
        hid_hi = sb("hid_hi", [P, FT, T], F32R, stack=phase)
        hid_lo = sb("hid_lo", [P, FT, T], F32R, stack=phase)
        conv = sb("conv", [P, 4, T], stack=phase)
        gated = sb("gated", [P, 2, T], stack=phase)
        hidden = sb("hidden", [P, 2, T], stack=phase)
        phase.close()
        phase = ExitStack()
        ot_hi = sb("ot_hi", [P, KT, T], F32R, stack=phase)
        ot_lo = sb("ot_lo", [P, KT, T], F32R, stack=phase)
        q2 = sb("q2", [P, KT, T], stack=phase)
        k2 = sb("k2", [P, KT, T], stack=phase)
        v2 = sb("v2", [P, 2, D], stack=phase)
        logit2 = sb("logit2", [P, 2, 3 * P], stack=phase)
        prob2 = sb("prob2", [P, 2, 3 * P], stack=phase)
        prob2_t = sb("prob2_t", [P, 2, 3 * P], stack=phase)
        h_sq = sb("h_sq", [P, 2 * T], stack=phase)
        h_a = sb("h_a", [P, 2 * T], stack=phase)
        h_y = sb("h_y", [P, 2 * T], stack=phase)
        h_t = sb("h_t", [P, 2 * T], stack=phase)
        phase.close()
        cgate, short, bprod = q2[:, 0:2, :], q2[:, 2:4, :], q2[:, 4:6, :]
        cu = q2[:, 6:8, :]

        bank = [ctx.enter_context(nc.psum_tensor(f"bank{n}", [P, 512], F32)) for n in range(8)]

        w_landed = [sem(f"w_landed{n}") for n in range(RAW)]
        hi_ready = sem("hi_ready")
        lo_ready = sem("lo_ready")
        unit_done = sem("unit_done")
        proj_free = sem("proj_free")
        ada_landed = [sem(f"ada_landed{n}") for n in range(2)]
        ada_used = sem("ada_used")
        ada_zero = sem("ada_zero")
        ada_red = sem("ada_red")
        mod_ready = sem("mod_ready")
        x_landed = sem("x_landed")
        v_landed = sem("v_landed")
        f_landed = sem("f_landed")
        fb_zero = sem("fb_zero")
        consts = sem("consts")
        x_turned = sem("x_turned")
        v_turned = sem("v_turned")
        vec_ready = sem("vec_ready")
        res_ready = sem("res_ready")
        sq_ready = sem("sq_ready")
        ss_ready = sem("ss_ready")
        na_ready = sem("na_ready")
        ln_ready = sem("ln_ready")
        y_ready = sem("y_ready")
        hx_ready = sem("hx_ready")
        h_hi = sem("h_hi")
        h_lo = sem("h_lo")
        wf_ready = sem("wf_ready")
        f_done = sem("f_done")
        f_act = sem("f_act")
        nlf_ready = sem("nlf_ready")
        cum_done = sem("cum_done")
        cum_ready = sem("cum_ready")
        v_ready = sem("v_ready")
        qk_ready = sem("qk_ready")
        score_done = sem("score_done")
        shift_ready = sem("shift_ready")
        p_ready = sem("p_ready")
        turn_done = sem("turn_done")
        pt_ready = sem("pt_ready")
        pv_done = sem("pv_done")
        z_ln = sem("z_ln")
        t_ready = sem("t_ready")
        lb_ready = sem("lb_ready")
        w_ready = sem("w_ready")
        a_ready = sem("a_ready")
        pad_zero = sem("pad_zero")
        o_fox = sem("o_fox")
        o_ready = sem("o_ready")
        oss_ready = sem("oss_ready")
        oln = sem("oln")
        oy = sem("oy")
        on_ready = sem("on_ready")
        ot_turned = sem("ot_turned")
        ot1_hi = sem("ot1_hi")
        ot1_lo = sem("ot1_lo")
        cv_lin = sem("cv_lin")
        tap1 = sem("tap1")
        gate_conv = sem("gate_conv")
        val_conv = sem("val_conv")
        sil_ready = sem("sil_ready")
        prod_ready = sem("prod_ready")
        hid_hi_r = sem("hid_hi_r")
        hid_lo_r = sem("hid_lo_r")
        qk_sq = sem("qk_sq")
        qk_ss = sem("qk_ss")
        qk_a = sem("qk_a")
        qk_ln = sem("qk_ln")
        qk_y = sem("qk_y")
        qk_norm = sem("qk_norm")
        v2_ready = sem("v2_ready")
        s2_done = sem("s2_done")
        m2_ready = sem("m2_ready")
        e2_ready = sem("e2_ready")
        p2_ready = sem("p2_ready")
        t2_done = sem("t2_done")
        pt2_ready = sem("pt2_ready")
        pv2_done = sem("pv2_done")
        o2_hi = sem("o2_hi")
        o2_lo = sem("o2_lo")
        cu_ready = sem("cu_ready")
        sc_lin = sem("sc_lin")
        sc_tap = sem("sc_tap")
        sc_out = sem("sc_out")
        sc_hi = sem("sc_hi")
        sc_lo = sem("sc_lo")
        dve_seq = sem("dve_seq")
        silu_r = sem("silu_r")
        out_turned = sem("out_turned")
        out_ready = [sem(f"out_ready{t}") for t in range(2)]
        stored = sem("stored")

        def unit(buf, u):
            return buf[:, u % SPLIT, :]

        def raw_half(c, h):
            return w_raw[:, c % RAW, h * UNIT:(h + 1) * UNIT]

        def vcol(tile, n, step=0, i=None):
            return vec[:, tile, cols(n, step, i, 1)]

        order1 = [("fv", 1024), ("fv", 1280), ("sv", 2568), ("sv", 2824), ("fq", 0), ("fk", 512), ("fq", 256),
                  ("fk", 768), ("sq", 1544), ("sk", 2056), ("sq", 1800), ("sk", 2312)]
        order2 = [("v", 2048), ("v", 2304), ("v", 2560), ("v", 2816), ("q", 0), ("k", 1024), ("q", 256),
                  ("k", 1280), ("q", 512), ("k", 1536), ("q", 768), ("k", 1792)]
        order3 = [(kind, base + CW * g) for g in range(4) for kind, base in (("c", D), ("u", 2 * D), ("b", 0))]

        def rows(a, k=None):
            a = a if k is None else a[:, k, :]
            return a.rearrange("a (k p) -> (a k) p", p=P)

        vectors = [(0, V_ATTN, rows(attn_norm_g)), (0, V_FOX, rows(fox_out_g)), (0, V_SB, rows(sb_out_g)),
                   (0, V_FFN, rows(ffn_norm_g)), (0, V_FINAL, final_norm_g.rearrange("(k p) -> k p", p=P)),
                   (0, V_MIX2, rows(norm_mix_2)), (0, V_FFN2, rows(norm_ffn_2)), (0, V_QG, q_gain_2),
                   (0, V_KG, k_gain_2), (0, V_C, rows(c_2)), (3, 0, rows(b_ada_2)),
                   (V_CONVB[0], V_CONVB[1], rows(conv_b))]
        vectors += [(0, V_CONV2 + KT * k, rows(conv_w_2, k)) for k in range(3)]
        vectors += [(*V_TAP[k], rows(conv_w, k)) for k in range(3)]

        block = ctx.enter_context(nc.Block())

        @block.sync
        def _(sp):
            def wide(w):
                return w.rearrange("(k p) n -> p k n", p=P)

            def load(c, src, i=None):
                if c >= RAW:
                    sp.wait_ge(lo_ready, at(2 * (c - RAW) + 2, 8, i))
                dst = w_raw[:, c % RAW, :].rearrange("p (k n) -> p k n", n=src.shape[2])
                sp.dma_start(dst, src).then_inc(w_landed[c % RAW], 16)

            def load_gated(c0, w, straight):
                def pair(c, p, i):
                    for n in range(2):
                        load(c + n, w[:, :, cols(n * FF + CW * p, 2 * CW, i, CW)], i)
                for p in range(straight):
                    pair(c0 + 2 * p, p, None)
                with sp.Fori(0, (PAIRS - straight) // 2) as i:
                    for j in range(2):
                        pair(c0 + 2 * (straight + j), straight + j, i)

            def load_down(c0, w):
                for d in range(3):
                    load(c0 + d, w[:, 2 * d:2 * d + 2, :])
                with sp.Fori(0, 2) as i:
                    for j in range(4):
                        load(c0 + 3 + j, w[:, cols(6 + 2 * j, 8, i, 2), :], i)

            for t in range(2):
                sp.dma_start(x_in[:, t, :], x[0, t * P:(t + 1) * P, :]).then_inc(x_landed, 16)
            w = wide(w_in[0])
            for n, (_, col) in enumerate(order1):
                load(IN1 + n, w[:, :, col:col + CW])
            w = wide(w_out[0])
            for n in range(4):
                load(OUT1 + n, w[:, :, n * CW:(n + 1) * CW])
            load_gated(UP1, wide(w_up[0]), 1)
            load_down(DOWN1, wide(w_down[0]))
            w = wide(w_qkv_2[0])
            for n, (_, col) in enumerate(order2):
                load(QKV + n, w[:, :, col:col + CW])
            w = wide(w_o_2[0])
            for n in range(4):
                load(OUT2 + n, w[:, :, n * CW:(n + 1) * CW])
            load_gated(UP2, wide(w_gate_up_2[0]), 3)
            load_down(DOWN2, wide(w_down_2[0]))
            w = wide(w_in_2[0])
            for n, (_, col) in enumerate(order3):
                load(IN3 + n, w[:, :, col:col + CW])
            w = wide(w_out_2[0])
            for n in range(4):
                load(OUT3 + n, w[:, :, n * CW:(n + 1) * CW])
            load_gated(UP3, wide(w_gate_up_2[1]), 1)
            load_down(DOWN3, wide(w_down_2[1]))
            for t in range(2):
                sp.wait_ge(out_ready[t], 2)
                sp.dma_start(out[0, t * P:(t + 1) * P, :], o_sb[:, t, :]).then_inc(stored, 16)
            sp.wait_ge(stored, 32)

        @block.gpsimd
        def _(pool):
            pool.memset(fbias[:], 0.0).then_inc(fb_zero, 1)
            pool.memset(ident[:], 0.0).then_inc(consts, 1)
            pool.memset(ones[:], 1.0).then_inc(consts, 1)
            pool.memset(upto[:], 1.0).then_inc(consts, 1)
            pool.memset(causal[:], 0.0).then_inc(consts, 1)
            pool.memset(later[:], -1.0).then_inc(consts, 1)
            pool.memset(minus[:], -1.0).then_inc(consts, 1)
            pool.memset(before[:], 1.0).then_inc(consts, 1)
            pool.wait_ge(consts, 7)
            pool.affine_select(ident[:], ident[:], [[-1, P]], ALU.not_equal, 1.0, base=0,
                               channel_multiplier=1).then_inc(consts, 1)
            pool.wait_ge(fb_zero, 1)
            pool.dma_start(fbias[0:1, :], forget_bias).then_inc(f_landed, 16)
            pool.dma_start(wf_raw[:], w_in[0].rearrange("(k p) n -> p k n", p=P)[:, :, 1536:1544]).then_inc(f_landed, 16)
            pool.affine_select(upto[:], upto[:], [[1, T]], ALU.is_ge, 0.0, base=0,
                               channel_multiplier=-1).then_inc(consts, 1)
            pool.affine_select(causal[:], causal[:], [[-1, T]], ALU.is_ge, NEG, base=P,
                               channel_multiplier=1).then_inc(consts, 1)
            pool.affine_select(later[:], later[:], [[-1, P]], ALU.is_gt, 0.0, base=0,
                               channel_multiplier=1).then_inc(consts, 1)
            for lo, n in ((0, T), (T, P)):
                pool.affine_select(before[:, lo:lo + n], before[:, lo:lo + n], [[1, n]], ALU.is_gt, 0.0, base=0,
                                   channel_multiplier=-1).then_inc(consts, 1)
            for l in range(2):
                if l:
                    pool.wait_ge(ada_red, l)
                for s in range(3):
                    pool.memset(ada_acc[:, s, :], 0.0).then_inc(ada_zero, 1)
                for s in range(3):
                    def fetch(i, j):
                        pool.dma_start(ada_raw[:, j, :], w_ada_2[l][cols(j * P, 2 * P, i, P), s * ADA_W:(s + 1) * ADA_W]
                                       ).then_inc(ada_landed[j], 16)
                    first = ADA * l + 8 * s
                    if first == 0:
                        fetch(None, 0)
                        fetch(None, 1)
                    with pool.Fori(int(first == 0), 4) as i:
                        for j in range(2):
                            pool.wait_ge(ada_used, at(first + j - 1, 2, i))
                            fetch(i, j)

        @block.scalar
        def _(act):
            def split(c, i=None):
                act.wait_ge(w_landed[c % RAW], at(16 * (c // RAW + 1), 16, i))
                for h in range(2):
                    split_unit(c, h, i)

            def split_unit(c, h, i=None):
                u = 2 * c + h
                if h == 0:
                    act.wait_ge(w_landed[c % RAW], at(16 * (c // RAW + 1), 16, i))
                if u >= SPLIT:
                    act.wait_ge(unit_done, at(u - SPLIT + 1, 8, i))
                act.activation(unit(w_hi, u), raw_half(c, h), ACT.Copy).then_inc(hi_ready, 1)

            def squares(n, version):
                for j in range(4):
                    act.wait_ge(res_ready, 4 * version + j + 1)
                    act.activation(scr[:, 2 * j:2 * j + 2, :], res[:, 2 * j:2 * j + 2, :],
                                   ACT.Square).then_inc(sq_ready, 1)

            def norm(n, m=None, shift=None):
                act.wait_ge(na_ready, n + 1)
                act.activation(n_y[:], n_a[:], ACT.Ln, scale=-2.0).then_inc(ln_ready, 1)
                act.wait_ge(ln_ready, n + 1)
                act.activation(n_y[:], n_y[:], ACT.Exp, scale=-0.5).then_inc(y_ready, 1)
                if m is None:
                    return
                for j in range(4):
                    act.wait_ge(hx_ready, 8 * m + 2 * j + 2)
                    if shift is None:
                        act.activation(act_hi[:, 2 * j:2 * j + 2, :], scr[:, 2 * j:2 * j + 2, :],
                                       ACT.Copy).then_inc(h_hi, 2)
                    else:
                        for k in (2 * j, 2 * j + 1):
                            act.activation(act_hi[:, k, :], scr[:, k, :], ACT.Identity,
                                           bias=shift(k)).then_inc(h_hi, 1)

            def gated_pair(c, pair, p, i, convolve):
                gate, val = bank[2 * (p % 2)], bank[2 * (p % 2) + 1]
                act.wait_ge(unit_done, at(2 * c + 4, 8, i))
                if convolve:
                    for q in range(4):
                        src = (gate, val)[q // 2][:, (q % 2) * T:(q % 2 + 1) * T]
                        f = (q // 2) * FT + 2 * p + q % 2
                        act.activation(conv[:, q, :], src, ACT.Identity, bias=vcol(2, 44 + f, 4, i),
                                       scale=vcol(2, f, 4, i)).then_inc(cv_lin, 1)
                    act.wait_ge(gate_conv, at(pair + 1, 2, i))
                    act.activation(gated[:], conv[:, 0:2, :], ACT.Silu).then_inc(sil_ready, 1)
                else:
                    act.activation(gated[:], gate[:].rearrange("p (t n) -> p t n", n=T), ACT.Silu
                                   ).then_inc(sil_ready, 1)
                act.wait_ge(prod_ready, at(pair + 1, 2, i))
                act.activation(hid_hi[:, cols(2 * p, 4, i, 2), :], hidden[:], ACT.Copy).then_inc(hid_hi_r, 1)

            def gated_layer(c0, pair0, straight, convolve):
                def step(c, pair, p, i):
                    split(c + 2, i)
                    split(c + 3, i)
                    gated_pair(c, pair, p, i, convolve)
                for p in range(straight):
                    step(c0 + 2 * p, pair0 + p, p, None)
                with act.Fori(0, (PAIRS - straight) // 2) as i:
                    for j in range(2):
                        p = straight + j
                        step(c0 + 2 * p, pair0 + p, p, i)

            def down_layer(c0):
                for d in range(3):
                    split(c0 + d + 2)
                if c0 == DOWN3:
                    for d in range(3, 9):
                        split(c0 + d + 2)
                    return
                with act.Fori(0, 2) as i:
                    for j in range(4):
                        split(c0 + 3 + j + 2, i)

            for tile, row, src in vectors:
                act.dma_start(v_in[row:row + src.shape[0], tile, :], src).then_inc(v_landed, 16)
            act.wait_ge(vec_ready, 1)
            act.activation(silu_c[:], vec[:, 0, V_C:V_C + KT], ACT.Silu).then_inc(silu_r, 1)
            squares(0, 0)
            act.wait_ge(f_landed, 32)
            act.activation(wf_hi[:], wf_raw[:], ACT.Copy).then_inc(wf_ready, 1)
            norm(0, 0)
            split(0)
            split(1)

            def fox_exp(h):
                act.wait_ge(shift_ready, h + 1)
                for t, (lo, hi) in enumerate(((0, P), (P, 3 * P))):
                    ins = act.activation(prob[:, h % 2, lo:hi], logit[:, h % 2, lo:hi], ACT.Exp,
                                         bias=nmax[:, h, t:t + 1], accum_out=rowsum[:, h, t:t + 1])
                ins.then_inc(p_ready, 1)

            def fox_turned(h):
                act.wait_ge(turn_done, h + 1)
                if h >= 2:
                    act.wait_ge(pv_done, h - 1)
                act.activation(prob_t[:, h % 2, :], bank[4 + h % 2][:, 0:3 * P], ACT.Copy).then_inc(pt_ready, 1)

            def stick_logs(h):
                b = sb_l[:, h % 2, :]
                act.wait_ge(score_done, 8 + h + 1)
                if h >= 2:
                    act.wait_ge(t_ready, h - 1)
                act.activation(b, bank[2 + h % 2][:, 0:3 * P], ACT.Abs).then_inc(z_ln, 1)
                act.wait_ge(z_ln, 3 * h + 1)
                act.activation(b, b, ACT.Exp, scale=-1.0).then_inc(z_ln, 1)
                act.wait_ge(z_ln, 3 * h + 2)
                act.activation(b, b, ACT.Ln, bias=1.0).then_inc(z_ln, 1)

            def stick_weights(h):
                act.wait_ge(w_ready, h + 1)
                b = sb_b[:, h % 2, :]
                act.activation(b, b, ACT.Exp).then_inc(a_ready, 1)

            def attend(s):
                if 1 <= s <= 8:
                    fox_turned(s - 1)
                if s < 8:
                    fox_exp(s)
                elif s < 16:
                    stick_logs(s - 8)
                if 9 <= s <= 16:
                    stick_weights(s - 9)

            for c in range(12):
                if c == 1:
                    act.wait_ge(f_done, 1)
                    act.activation(f_abs[:], bank[2][:, 0:16].rearrange("p (t n) -> p t n", n=8), ACT.Abs
                                   ).then_inc(f_act, 1)
                if c == 2:
                    act.wait_ge(f_act, 1)
                    act.activation(f_log[:], f_abs[:], ACT.Exp, scale=-1.0).then_inc(f_act, 1)
                    act.wait_ge(f_act, 2)
                    act.activation(f_log[:], f_log[:], ACT.Ln, bias=1.0).then_inc(f_act, 1)
                for h in range(2):
                    split_unit(c + 2, h)
                    if c >= 6:
                        attend(2 * (c - 6) + h)
            for s in range(12, 18):
                attend(s)

            act.wait_ge(o_ready, 1)
            for t in range(2):
                for g in range(2):
                    ins = act.activation(q_pad[:, 4 * t + 2 * g:4 * t + 2 * g + 2, :].rearrange("p h n -> p (h n)"),
                                         o_tok[:, t, g * 512:(g + 1) * 512], ACT.Square,
                                         accum_out=small[:, 0, 2 * t + g:2 * t + g + 1])
            ins.then_inc(oss_ready, 1)
            act.wait_ge(oln, 1)
            act.activation(small[:, 2, 0:4], small[:, 1, 0:4], ACT.Ln, scale=-2.0).then_inc(oln, 1)
            act.wait_ge(oln, 2)
            act.activation(small[:, 3, 0:4], small[:, 2, 0:4], ACT.Exp, scale=-0.5).then_inc(oy, 1)
            for j in range(4):
                act.wait_ge(ot_turned, j + 1)
                for k in (2 * j, 2 * j + 1):
                    act.activation(act_hi[:, k, :], bank[2 + j][:, (k % 2) * T:(k % 2 + 1) * T], ACT.Copy,
                                   scale=vcol(0, V_FOX + k)).then_inc(ot1_hi, 1)
            for n in range(4):
                split(OUT1 + n + 2)
            squares(1, 1)
            norm(1, 1)
            gated_layer(UP1, 0, 1, True)
            down_layer(DOWN1)
            squares(2, 2)
            norm(2)

            squares(3, 3)
            norm(3, 2, shift=lambda k: mod[:, 0, SH_M + k:SH_M + k + 1])

            def head_squares(n):
                c = 4 + n
                act.wait_ge(unit_done, 2 * (QKV + c) + 2)
                src = bank[c % 2][:, :]
                if n:
                    act.wait_ge(qk_ss, n)
                act.activation(h_sq[:], src, ACT.Square)
                dst = (q2, k2)[n % 2][:, 2 * (n // 2):2 * (n // 2) + 2, :]
                act.activation(dst, src.rearrange("p (t n) -> p t n", n=T), ACT.Copy).then_inc(qk_sq, 1)

            def head_rms(n):
                act.wait_ge(qk_a, n + 1)
                act.activation(h_y[:], h_a[:], ACT.Ln, scale=-2.0).then_inc(qk_ln, 1)
                act.wait_ge(qk_ln, n + 1)
                act.activation(h_y[:], h_y[:], ACT.Exp, scale=-0.5).then_inc(qk_y, 1)

            def attend2(s):
                if 1 <= s <= 8:
                    h = s - 1
                    act.wait_ge(t2_done, h + 1)
                    if h >= 2:
                        act.wait_ge(pv2_done, h - 1)
                    act.activation(prob2_t[:, h % 2, :], bank[4][:, 0:3 * P], ACT.Copy).then_inc(pt2_ready, 1)
                if s < 8:
                    act.wait_ge(m2_ready, s + 1)
                    for t, (lo, hi) in enumerate(((0, P), (P, 3 * P))):
                        ins = act.activation(prob2[:, s % 2, lo:hi], logit2[:, s % 2, lo:hi], ACT.Exp,
                                             bias=nmax[:, s, t:t + 1], accum_out=rowsum[:, s, t:t + 1])
                    ins.then_inc(e2_ready, 1)
                if s >= 2:
                    h = s - 2
                    act.wait_ge(pv2_done, h + 1)
                    act.activation(ot_hi[:, h, :], bank[5 + h % 2][:, 0:T], ACT.Copy).then_inc(o2_hi, 1)

            for c in range(12):
                split_unit(QKV + c + 2, 0)
                if c >= 5:
                    head_rms(c - 5)
                split_unit(QKV + c + 2, 1)
                if c >= 4:
                    head_squares(c - 4)
                if c >= 6:
                    attend2(c - 6)
            head_rms(7)
            for s in range(6, 10):
                attend2(s)
            for n in range(4):
                split(OUT2 + n + 2)
            squares(4, 4)
            norm(4, 3, shift=lambda k: mod[:, 0, SH_F + k:SH_F + k + 1])
            gated_layer(UP2, PAIRS, 3, False)
            down_layer(DOWN2)

            squares(5, 5)
            norm(5, 4, shift=lambda k: mod[:, 1, SH_M + k:SH_M + k + 1])
            for c in range(12):
                split(IN3 + c + 2)
                g = c // 3
                if c % 3 == 1:
                    act.wait_ge(cu_ready, g + 1)
                    for t in range(2):
                        act.activation(short[:, t, :], cu[:, t, :], ACT.Identity, bias=0.0,
                                       scale=vcol(0, V_CONV2 + 2 * KT + 2 * g + t)).then_inc(sc_lin, 1)
                if c % 3 == 2:
                    act.wait_ge(sc_out, g + 1)
                    act.activation(ot_hi[:, 2 * g:2 * g + 2, :], bprod, ACT.Copy).then_inc(sc_hi, 1)
            for n in range(4):
                split(OUT3 + n + 2)
            squares(6, 6)
            norm(6, 5, shift=lambda k: mod[:, 1, SH_F + k:SH_F + k + 1])
            gated_layer(UP3, 2 * PAIRS, 1, False)
            down_layer(DOWN3)
            for t in range(2):
                act.wait_ge(out_turned, 2 * t + 1)
                act.activation(o_sb[:, t, 0:512], bank[2 * t][:, :], ACT.Copy).then_inc(out_ready[t], 1)

        @block.vector
        def _(dve):
            seq = [0]

            def link(ins):
                seq[0] += 1
                ins.then_inc(dve_seq, 1)
                dve.wait_ge(dve_seq, seq[0])

            def split_unit(c, h, i=None):
                u = 2 * c + h
                dve.wait_ge(hi_ready, at(u + 1, 8, i))
                dve.tensor_tensor(unit(w_lo, u), raw_half(c, h), unit(w_hi, u).bitcast(F32),
                                  ALU.subtract).then_inc(lo_ready, 1)

            def split(c, i=None):
                for h in range(2):
                    split_unit(c, h, i)

            def ada(n, i=None):
                s, k = n % ADA // 8, n % 8
                if n % 8 == 0 or i is not None:
                    dve.wait_ge(ada_zero, 3 * (n // ADA) + s + 1)
                dve.wait_ge(ada_landed[n % 2], at(16 * (n // 2 + 1), 8 * ada_step[0], i))
                if n == 0:
                    dve.wait_ge(silu_r, 1)
                else:
                    dve.wait_ge(ada_used, at(n, ada_step[0], i))
                dve.scalar_tensor_tensor(ada_acc[:, s, :], ada_raw[:, n % 2, :], silu_c[:, cols(k, ada_step[0], i, 1)],
                                         ada_acc[:, s, :], ALU.mult, ALU.add).then_inc(ada_used, 1)
            ada_step = [4]

            def norm(n, gain, shift=None, version=None):
                dve.wait_ge(ss_ready, n + 1)
                dve.tensor_scalar(n_a[:], bank[2][:, 0:T], -0.5 / D, -0.5 * EPS, ALU.mult,
                                  ALU.add).then_inc(na_ready, 1)
                dve.wait_ge(y_ready, n + 1)
                link(dve.tensor_tensor(n_t[:], n_y[:], n_y[:], ALU.mult))
                link(dve.tensor_tensor(n_t[:], n_t[:], n_a[:], ALU.mult))
                link(dve.scalar_tensor_tensor(rstd[:], n_t[:], 1.5, n_y[:], ALU.add, ALU.mult))

                def part(k):
                    dst = scr if version is None else res
                    ins = dve.scalar_tensor_tensor(dst[:, k, :], res[:, k, :], gain(k), rstd[:], ALU.mult, ALU.mult)
                    if version is None:
                        ins.then_inc(hx_ready, 1)
                    elif k % 2:
                        ins.then_inc(res_ready, 1)

                def rest(j):
                    dve.wait_ge(h_hi, 8 * hn[0] + 2 * j + 2)
                    pair = slice(2 * j, 2 * j + 2)
                    if shift is None:
                        dve.tensor_tensor(act_lo[:, pair, :], scr[:, pair, :], act_hi[:, pair, :].bitcast(F32),
                                          ALU.subtract).then_inc(h_lo, 1)
                    else:
                        for k in (2 * j, 2 * j + 1):
                            ins = dve.scalar_tensor_tensor(act_lo[:, k, :], scr[:, k, :], shift(k),
                                                           act_hi[:, k, :].bitcast(F32), ALU.add, ALU.subtract)
                        ins.then_inc(h_lo, 1)
                for j in range(4):
                    part(2 * j)
                    part(2 * j + 1)
                    if version is None and j:
                        rest(j - 1)
                if version is None:
                    rest(3)
                    hn[0] += 1
            hn = [0]

            def add_up(c0, first, gate=None):
                for n in range(4):
                    split(c0 + n + 2)
                    if first is not None:
                        ada(first + n)
                    dve.wait_ge(unit_done, 2 * (c0 + n) + 2)
                    update(bank[proj(c0 + n) % 2], n, gate, proj_free)

            def update(src, j, gate, free):
                pair = slice(2 * j, 2 * j + 2)
                if gate is None:
                    link(dve.tensor_tensor(res[:, pair, :], src[:].rearrange("p (t n) -> p t n", n=T), res[:, pair, :],
                                           ALU.add))
                else:
                    for t in range(2):
                        k = 2 * j + t
                        ins = dve.scalar_tensor_tensor(res[:, k, :], src[:, t * T:(t + 1) * T], gate(k), res[:, k, :],
                                                       ALU.mult, ALU.add)
                    link(ins)
                dve.sem_inc(res_ready, 1)
                if free is not None:
                    dve.sem_inc(free, 1)

            def gated_pair(c, pair, p, i, convolve):
                gate, val = bank[2 * (p % 2)], bank[2 * (p % 2) + 1]
                if convolve:
                    for half, (src, done) in enumerate(((gate, gate_conv), (val, val_conv))):
                        dve.wait_ge(cv_lin, at(4 * pair + 2 * half + 2, 8, i))
                        for tap in (1, 0):
                            lag = 2 - tap
                            for q in (2 * half, 2 * half + 1):
                                tile, base = V_TAP[tap]
                                f = half * FT + 2 * p + q % 2
                                if tap == 0:
                                    dve.wait_ge(tap1, at(4 * pair + q + 1, 8, i))
                                ins = dve.scalar_tensor_tensor(conv[:, q, lag:T], src[:, (q % 2) * T:(q % 2 + 1) * T - lag],
                                                               vcol(tile, base + f, 4, i), conv[:, q, lag:T],
                                                               ALU.mult, ALU.add)
                                if tap == 1:
                                    ins.then_inc(tap1, 1)
                        ins.then_inc(done, 1)
                    dve.wait_ge(val_conv, at(pair + 1, 2, i))
                    value = conv[:, 2:4, :]
                else:
                    value = val[:].rearrange("p (t n) -> p t n", n=T)
                dve.wait_ge(sil_ready, at(pair + 1, 2, i))
                if pair or i is not None:
                    dve.wait_ge(hid_lo_r, at(pair, 2, i))
                dve.tensor_tensor(hidden[:], value, gated[:], ALU.mult).then_inc(prod_ready, 1)
                dve.wait_ge(hid_hi_r, at(pair + 1, 2, i))
                kt = cols(2 * p, 4, i, 2)
                dve.tensor_tensor(hid_lo[:, kt, :], hidden[:], hid_hi[:, kt, :].bitcast(F32),
                                  ALU.subtract).then_inc(hid_lo_r, 1)

            def gated_layer(c0, pair0, straight, convolve, ada0=None):
                def step(c, pair, p, i, j=None):
                    split(c + 2, i)
                    split(c + 3, i)
                    if ada0 is not None and i is not None:
                        ada(ada0 + j, i)
                    gated_pair(c, pair, p, i, convolve)
                for p in range(straight):
                    step(c0 + 2 * p, pair0 + p, p, None)
                ada_step[0] = 2
                with dve.Fori(0, (PAIRS - straight) // 2) as i:
                    for j in range(2):
                        p = straight + j
                        step(c0 + 2 * p, pair0 + p, p, i, j)
                ada_step[0] = 4

            def down_layer(c0, ada0, gate):
                for d in range(3):
                    split(c0 + d + 2)
                if c0 == DOWN3:
                    for d in range(3, 9):
                        split(c0 + d + 2)
                else:
                    with dve.Fori(0, 2) as i:
                        for j in range(4):
                            split(c0 + 3 + j + 2, i)
                            ada(ada0 + j, i)
                dve.wait_ge(unit_done, 2 * (c0 + 11))
                for j in range(4):
                    update(bank[4 + j], j, gate, None)

            def modulation(l):
                dve.wait_ge(ada_red, l + 1)
                link(dve.tensor_tensor(mod[:, l, :], bank[1][:, 0:6 * KT], vec[:, 3, 6 * KT * l:6 * KT * (l + 1)], ALU.add))
                for n, (sc, g) in enumerate(((SC_M, V_MIX2), (SC_F, V_FFN2))):
                    ins = dve.scalar_tensor_tensor(gain2[:, 2 * l + n, :], mod[:, l, sc:sc + KT], 1.0,
                                                   vec[:, 0, g + KT * l:g + KT * (l + 1)], ALU.add, ALU.mult)
                link(ins)
                dve.sem_inc(mod_ready, 1)

            for n in range(4):
                dve.wait_ge(v_turned, n + 1)
                dve.tensor_copy(vec[:, n, 0:ROWS[n]], bank[V_BANKS[n]][:, 0:ROWS[n]]).then_inc(vec_ready, 1)
            for j in range(4):
                dve.wait_ge(x_turned, j + 1)
                dve.tensor_copy(res[:, 2 * j:2 * j + 2, :], bank[X_BANKS[j]][:].rearrange("p (t n) -> p t n", n=T)
                                ).then_inc(res_ready, 1)
            dve.wait_ge(vec_ready, 4)
            dve.tensor_scalar(qk_gain[:, 0:1], vec[:, 0, V_QG:V_QG + 1], float(P) ** -0.5, None, ALU.mult)
            dve.tensor_copy(qk_gain[:, 1:2], vec[:, 0, V_KG:V_KG + 1])
            dve.wait_ge(wf_ready, 1)
            dve.tensor_tensor(wf_lo[:], wf_raw[:], wf_hi[:].bitcast(F32), ALU.subtract).then_inc(wf_ready, 1)
            dve.wait_ge(res_ready, 4)
            norm(0, lambda k: vcol(0, V_ATTN + k))
            split(0)
            split(1)
            dve.wait_ge(h_lo, 4)
            for half in range(2):
                rows = slice(64 * (1 - half), 64 * (2 - half))
                dve.memset(q_pad[rows, half:8:2, :], 0.0).then_inc(pad_zero, 1)
                dve.memset(k_pad[rows, half:8:2, :], 0.0).then_inc(pad_zero, 1)

            def place(c):
                kind, col = order1[c]
                n = 0 if c % 2 == 0 or kind[1] != "v" else 1
                g = (c - 4) // 2 % 2
                src = bank[c % 2][:].rearrange("p (t n) -> p t n", n=T)
                dve.wait_ge(unit_done, 2 * c + 2)
                if kind[1] == "v":
                    base = (0 if kind[0] == "f" else 512) + CW * n
                    dve.tensor_copy(v_tok[:, :, base:base + CW], src).then_inc(proj_free, 1)
                elif kind == "fk":
                    dve.tensor_copy(k_fox[:, 2 * g:2 * g + 2, :], src).then_inc(proj_free, 1)
                elif kind == "sq":
                    dve.tensor_scalar(q_sb[:, 2 * g:2 * g + 2, :], src, 0.125, None, ALU.mult).then_inc(proj_free, 1)
                else:
                    pad, scale = (q_pad, 0.125) if kind == "fq" else (k_pad, 1.0)
                    for half in range(2):
                        rows = slice(64 * half, 64 * half + 64)
                        ins = dve.tensor_scalar(pad[rows, 4 * g + half:4 * g + 4:2, :], src[rows], scale, None, ALU.mult)
                    ins.then_inc(proj_free, 1)

            def fox_shift(h):
                dve.wait_ge(score_done, h + 1)
                s = bank[2 + h % 2]
                if h == 0:
                    dve.wait_ge(consts, 13)
                if h >= 2:
                    dve.wait_ge(p_ready, h - 1)
                dve.scalar_tensor_tensor(logit[:, h % 2, 0:P], s[:, 0:P], f_cum[:, 0, h:h + 1], causal[:, P:T],
                                         ALU.add, ALU.add)
                link(dve.scalar_tensor_tensor(logit[:, h % 2, P:3 * P], s[:, P:3 * P], f_cum[:, 1, h:h + 1], causal[:],
                                              ALU.add, ALU.add))
                dve.tensor_reduce(nmax[:, h, 0:1], logit[:, h % 2, 0:P], AX.X, ALU.max, negate=True)
                dve.tensor_reduce(nmax[:, h, 1:2], logit[:, h % 2, P:3 * P], AX.X, ALU.max,
                                  negate=True).then_inc(shift_ready, 1)

            def stick_parts(h):
                z = bank[2 + h % 2][:, 0:3 * P]
                dve.wait_ge(z_ln, 3 * h + 3)
                link(dve.scalar_tensor_tensor(sb_t[:], z, 0.0, sb_l[:, h % 2, :], ALU.max, ALU.add))
                if h >= 2:
                    dve.wait_ge(turn_done, 8 + h - 1)
                dve.tensor_tensor(sb_m[:, h % 2, :], sb_t[:], before[:], ALU.mult).then_inc(t_ready, 1)
                if h >= 2:
                    dve.wait_ge(pv_done, 8 + h - 1)
                dve.tensor_tensor(sb_b[:, h % 2, :], z, sb_t[:], ALU.subtract).then_inc(lb_ready, 1)

            def stick_sum(h):
                dve.wait_ge(turn_done, 8 + h + 1)
                dve.wait_ge(lb_ready, h + 1)
                b = sb_b[:, h % 2, :]
                dve.tensor_tensor(b, bank[4 + h % 2][:, 0:3 * P], b, ALU.add).then_inc(w_ready, 1)

            def stick_mask(h):
                dve.wait_ge(a_ready, h + 1)
                b = sb_b[:, h % 2, :]
                dve.tensor_tensor(b, b, before[:], ALU.mult).then_inc(pt_ready, 1)

            def outputs(g):
                dve.wait_ge(pv_done, 8 * g + 8)
                for t in range(2):
                    dst = o_tok[:, t, 512 * g:512 * (g + 1)]
                    if g == 0:
                        ins = dve.tensor_tensor(dst.rearrange("p (h d) -> p h d", d=64),
                                                bank[6 + t][:].rearrange("p (h d) -> p h d", d=64),
                                                rinv[:, 0:8, t:t + 1].broadcast_to([P, 8, 64]), ALU.mult)
                    else:
                        ins = dve.tensor_copy(dst, bank[6 + t][:])
                ins.then_inc(o_fox if g == 0 else o_ready, 1)

            def attend(s):
                if s < 8:
                    fox_shift(s)
                if 9 <= s <= 16:
                    stick_sum(s - 9)
                if 8 <= s < 16:
                    stick_parts(s - 8)
                if 9 <= s <= 16:
                    stick_mask(s - 9)
                if s == 9:
                    dve.wait_ge(p_ready, 8)
                    link(dve.reciprocal(rinv[:, 0:8, :], rowsum[:, 0:8, :]))
                    outputs(0)
                if s == 17:
                    outputs(1)

            for c in range(12):
                if c == 2:
                    dve.wait_ge(f_act, 3)
                    dve.tensor_tensor(nlf[:], f_neg[:], f_log[:], ALU.add).then_inc(nlf_ready, 1)
                for h in range(2):
                    split_unit(c + 2, h)
                    if h == 0 and c < 12:
                        ada(c)
                    if h == 1:
                        place(c)
                        if c == 1:
                            f = bank[2][:, 0:16].rearrange("p (t n) -> p t n", n=8)
                            dve.wait_ge(f_act, 1)
                            link(dve.tensor_scalar(f_neg[:], f, -1.0, 0.0, ALU.mult, ALU.max))
                        if c == 3:
                            dve.wait_ge(cum_done, 1)
                            dve.tensor_scalar(f_cum[:], bank[2][:, 16:32].rearrange("p (t n) -> p t n", n=8), -1.0, None,
                                              ALU.mult).then_inc(cum_ready, 1)
                    if c >= 6:
                        attend(2 * (c - 6) + h)
            for s in range(12, 18):
                attend(s)
            dve.wait_ge(oss_ready, 1)
            dve.tensor_scalar(small[:, 1, 0:4], small[:, 0, 0:4], -0.5 / 512, -0.5 * EPS, ALU.mult, ALU.add).then_inc(oln, 1)
            dve.wait_ge(oy, 1)
            y = small[:, 3, 0:4]
            link(dve.tensor_tensor(small[:, 4, 0:4], y, y, ALU.mult))
            link(dve.tensor_tensor(small[:, 4, 0:4], small[:, 4, 0:4], small[:, 1, 0:4], ALU.mult))
            link(dve.scalar_tensor_tensor(small[:, 5, 0:4], small[:, 4, 0:4], 1.5, y, ALU.add, ALU.mult))
            for g in range(2):
                for t in range(2):
                    o = o_tok[:, t, g * 512:(g + 1) * 512]
                    dve.tensor_scalar(o, o, small[:, 5, 2 * t + g:2 * t + g + 1], None, ALU.mult).then_inc(on_ready, 1)
            for j in range(4):
                dve.wait_ge(ot1_hi, 2 * j + 2)
                for k in (2 * j, 2 * j + 1):
                    ins = dve.scalar_tensor_tensor(act_lo[:, k, :], bank[2 + j][:, (k % 2) * T:(k % 2 + 1) * T],
                                                   vcol(0, V_FOX + k), act_hi[:, k, :].bitcast(F32), ALU.mult, ALU.subtract)
                ins.then_inc(ot1_lo, 1)
            add_up(OUT1, 12)
            norm(1, lambda k: vcol(0, V_FFN + k))
            gated_layer(UP1, 0, 1, True)
            down_layer(DOWN1, 16, None)
            norm(2, lambda k: vcol(0, V_FINAL + k), version=3)

            modulation(0)
            norm(3, lambda k: gain2[:, 0, k:k + 1], shift=lambda k: mod[:, 0, SH_M + k:SH_M + k + 1])

            def head_norm(n):
                dve.wait_ge(qk_ss, n + 1)
                dve.tensor_scalar(h_a[:], bank[7][:], -0.5 / P, -0.5 * EPS, ALU.mult, ALU.add).then_inc(qk_a, 1)
                dve.wait_ge(qk_a, n + 1)
                dve.sem_inc(proj_free, 1)
                dve.wait_ge(qk_y, n + 1)
                link(dve.tensor_tensor(h_t[:], h_y[:], h_y[:], ALU.mult))
                link(dve.tensor_tensor(h_t[:], h_t[:], h_a[:], ALU.mult))
                link(dve.scalar_tensor_tensor(h_t[:], h_t[:], 1.5, h_y[:], ALU.add, ALU.mult))
                dst = (q2, k2)[n % 2][:, 2 * (n // 2):2 * (n // 2) + 2, :]
                dve.scalar_tensor_tensor(dst, dst, qk_gain[:, n % 2:n % 2 + 1], h_t[:].rearrange("p (t n) -> p t n", n=T),
                                         ALU.mult, ALU.mult).then_inc(qk_norm, 1)

            def attend2(s):
                if s < 8:
                    dve.wait_ge(s2_done, s + 1)
                    b = bank[2 + s % 2]
                    dve.tensor_tensor(logit2[:, s % 2, 0:P], b[:, 0:P], causal[:, P:T], ALU.add)
                    link(dve.tensor_tensor(logit2[:, s % 2, P:3 * P], b[:, P:3 * P], causal[:], ALU.add))
                    dve.tensor_reduce(nmax[:, s, 0:1], logit2[:, s % 2, 0:P], AX.X, ALU.max, negate=True)
                    dve.tensor_reduce(nmax[:, s, 1:2], logit2[:, s % 2, P:3 * P], AX.X, ALU.max,
                                      negate=True).then_inc(m2_ready, 1)
                if s >= 2:
                    h = s - 2
                    dve.wait_ge(o2_hi, h + 1)
                    dve.tensor_tensor(ot_lo[:, h, :], bank[5 + h % 2][:, 0:T], ot_hi[:, h, :].bitcast(F32),
                                      ALU.subtract).then_inc(o2_lo, 1)
                if s < 8:
                    dve.wait_ge(e2_ready, s + 1)
                    link(dve.reciprocal(rinv[:, s, :], rowsum[:, s, :]))
                    for t, (lo, hi) in enumerate(((0, P), (P, 3 * P))):
                        ins = dve.tensor_scalar(prob2[:, s % 2, lo:hi], prob2[:, s % 2, lo:hi], rinv[:, s, t:t + 1], None,
                                                ALU.mult)
                    ins.then_inc(p2_ready, 1)

            for c in range(12):
                split_unit(QKV + c + 2, 0)
                if c >= 5:
                    head_norm(c - 5)
                split_unit(QKV + c + 2, 1)
                if c < 4:
                    dve.wait_ge(unit_done, 2 * (QKV + c) + 2)
                    dve.tensor_copy(v2[:, :, CW * c:CW * (c + 1)], bank[c % 2][:].rearrange("p (t n) -> p t n", n=T)
                                    ).then_inc(proj_free, 1)
                    ada(ADA + c)
                if c >= 6:
                    attend2(c - 6)
            head_norm(7)
            for s in range(6, 10):
                attend2(s)
            add_up(OUT2, ADA + 4, lambda k: mod[:, 0, G_M + k:G_M + k + 1])
            norm(4, lambda k: gain2[:, 1, k:k + 1], shift=lambda k: mod[:, 0, SH_F + k:SH_F + k + 1])
            gated_layer(UP2, PAIRS, 3, False, ADA + 8)
            down_layer(DOWN2, ADA + 16, lambda k: mod[:, 0, G_F + k:G_F + k + 1])

            modulation(1)
            norm(5, lambda k: gain2[:, 2, k:k + 1], shift=lambda k: mod[:, 1, SH_M + k:SH_M + k + 1])
            for c in range(12):
                split(IN3 + c + 2)
                g = c // 3
                src = bank[c % 2][:].rearrange("p (t n) -> p t n", n=T)
                dve.wait_ge(unit_done, 2 * (IN3 + c) + 2)
                if c % 3 == 0:
                    link(dve.tensor_copy(cgate, src))
                    dve.sem_inc(proj_free, 1)
                elif c % 3 == 1:
                    dve.tensor_tensor(cu, src, cgate, ALU.mult).then_inc(cu_ready, 1)
                    dve.wait_ge(cu_ready, g + 1)
                    dve.sem_inc(proj_free, 1)
                    for tap in (1, 0):
                        lag = 2 - tap
                        for t in range(2):
                            if tap == 1:
                                dve.wait_ge(sc_lin, 2 * g + t + 1)
                            else:
                                dve.wait_ge(sc_tap, 4 * g + t + 1)
                            dve.scalar_tensor_tensor(short[:, t, lag:T], cu[:, t, 0:T - lag],
                                                     vcol(0, V_CONV2 + KT * tap + 2 * g + t), short[:, t, lag:T],
                                                     ALU.mult, ALU.add).then_inc(sc_tap, 1)
                else:
                    dve.wait_ge(sc_tap, 4 * g + 4)
                    dve.tensor_tensor(bprod, src, short, ALU.mult).then_inc(sc_out, 1)
                    dve.wait_ge(sc_out, g + 1)
                    dve.sem_inc(proj_free, 1)
                    dve.wait_ge(sc_hi, g + 1)
                    pair = slice(2 * g, 2 * g + 2)
                    dve.tensor_tensor(ot_lo[:, pair, :], bprod, ot_hi[:, pair, :].bitcast(F32),
                                      ALU.subtract).then_inc(sc_lo, 1)
            add_up(OUT3, None, lambda k: mod[:, 1, G_M + k:G_M + k + 1])
            norm(6, lambda k: gain2[:, 3, k:k + 1], shift=lambda k: mod[:, 1, SH_F + k:SH_F + k + 1])
            gated_layer(UP3, 2 * PAIRS, 1, False)
            down_layer(DOWN3, None, lambda k: mod[:, 1, G_F + k:G_F + k + 1])
            for t in range(2):
                dve.wait_ge(out_turned, 2 * t + 2)
                dve.tensor_copy(o_sb[:, t, 512:D], bank[2 * t + 1][:, :]).then_inc(out_ready[t], 1)

        @block.tensor
        def _(pe):
            def products(dst, a_hi, a_lo, b_hi, b_lo, start, stop):
                pe.matmul(dst, a_hi, b_hi, start=start, stop=False, skip_group_check=True)
                pe.matmul(dst, a_hi, b_lo, start=False, stop=False, skip_group_check=True)
                return pe.matmul(dst, a_lo, b_hi, start=False, stop=stop, skip_group_check=True)

            def half_chunk(c, h, dst, src_hi, src_lo, i=None, ready=None, moving=False):
                u = 2 * c + h
                pe.wait_ge(lo_ready, at(u + 1, 8, i))
                whi, wlo = unit(w_hi, u), unit(w_lo, u)
                for k in range(4 * h, 4 * h + 4):
                    if ready is not None:
                        ready(k)
                    for t in range(2):
                        o = dst[:, t * T:(t + 1) * T]
                        first, last = k == 0 and t == 0, k == KT - 1
                        if moving:
                            w = slice((k % 4) * CW, (k % 4 + 1) * CW)
                            tok = slice(t * P, (t + 1) * P)
                            ins = products(o, src_hi[:, k, tok], src_lo[:, k, tok], whi[:, w], wlo[:, w], first, last)
                        else:
                            w = slice((k % 4) * CW + t * P, (k % 4) * CW + (t + 1) * P)
                            ins = products(o, whi[:, w], wlo[:, w], src_hi[:, k, :], src_lo[:, k, :], first, last)
                ins.then_inc(unit_done, 1)

            def chunk(c, dst, src_hi, src_lo, i=None, ready=None):
                for h in range(2):
                    half_chunk(c, h, dst, src_hi, src_lo, i, ready)

            def bank_free(c):
                if proj(c) >= 2:
                    pe.wait_ge(proj_free, proj(c) - 1)

            def operand(n):
                return lambda k: pe.wait_ge(h_lo, 4 * n + k // 2 + 1) if k % 2 == 0 else None

            def square_sums(n):
                for j in range(4):
                    pe.wait_ge(sq_ready, 4 * n + j + 1)
                    for k in (2 * j, 2 * j + 1):
                        ins = pe.matmul(bank[2][:, 0:T], ones[:], scr[:, k, :], start=k == 0, stop=k == KT - 1)
                ins.then_inc(ss_ready, 1)

            def gated_layer(c0, pair0, straight, norm_no):
                def step(c, pair, p, i, ready=None):
                    if pair > 1 or i is not None:
                        pe.wait_ge(prod_ready, at(pair - 1, 2, i))
                    chunk(c, bank[2 * (p % 2)], act_hi, act_lo, i, ready)
                    chunk(c + 1, bank[2 * (p % 2) + 1], act_hi, act_lo, i)
                for p in range(straight):
                    step(c0 + 2 * p, pair0 + p, p, None, operand(norm_no) if p == 0 else None)
                with pe.Fori(0, (PAIRS - straight) // 2) as i:
                    for j in range(2):
                        p = straight + j
                        step(c0 + 2 * p, pair0 + p, p, i)

            def down_layer(c0, pair0):
                def rows(d, i=None):
                    pe.wait_ge(hid_lo_r, at(pair0 + d + 1, 4, i))
                    for h in range(2):
                        u = 2 * (c0 + d) + h
                        pe.wait_ge(lo_ready, at(u + 1, 8, i))
                        kt = 2 * d + h
                        for o in range(KT):
                            w = slice(o * P, (o + 1) * P)
                            ins = products(bank[4 + o // 2][:, (o % 2) * T:(o % 2 + 1) * T], unit(w_hi, u)[:, w],
                                           unit(w_lo, u)[:, w], hid_hi[:, cols(kt, 8, i, 1), :], hid_lo[:, cols(kt, 8, i, 1), :],
                                           kt == 0 and o % 2 == 0, False)
                        ins.then_inc(unit_done, 1)
                for d in range(3):
                    rows(d)
                with pe.Fori(0, 2) as i:
                    for j in range(4):
                        rows(3 + j, i)

            def mod_sums(l):
                pe.wait_ge(ada_used, ADA * (l + 1))
                for m in range(6 * KT):
                    s, o = m // 16, (m % 16) * P
                    ins = pe.matmul(bank[1][:, m:m + 1], ada_acc[:, s, o:o + P], ones[:, 0:1], start=True, stop=True)
                ins.then_inc(ada_red, 1)

            pe.wait_ge(consts, 8)
            pe.wait_ge(v_landed, 16 * len(vectors))
            for n in range(4):
                pe.transpose(bank[V_BANKS[n]][:, 0:ROWS[n]], v_in[0:ROWS[n], n, :], ident[0:ROWS[n], 0:ROWS[n]]
                             ).then_inc(v_turned, 1)
            pe.wait_ge(x_landed, 32)
            for j in range(4):
                for n in range(4):
                    k, t = 2 * j + n // 2, n % 2
                    ins = pe.transpose(bank[X_BANKS[j]][:, n * P:(n + 1) * P], x_in[:, t, k * P:(k + 1) * P], ident[:])
                ins.then_inc(x_turned, 1)
            square_sums(0)

            def forget_logits():
                pe.wait_ge(wf_ready, 2)
                pe.wait_ge(f_landed, 32)
                for t in range(2):
                    o = bank[2][:, 8 * t:8 * t + 8]
                    tok = slice(t * P, (t + 1) * P)
                    for k in range(KT):
                        products(o, act_hi[:, k, tok], act_lo[:, k, tok], wf_hi[:, k, :], wf_lo[:, k, :],
                                 t == 0 and k == 0, False)
                    ins = pe.matmul(o, ones[:], fbias[:], start=False, stop=True, skip_group_check=True)
                ins.then_inc(f_done, 1)

            def forget_sums():
                pe.wait_ge(nlf_ready, 1)
                pe.wait_ge(consts, 13)
                pe.matmul(bank[2][:, 16:24], upto[:, 0:P], nlf[:, 0, :], start=True, stop=True, skip_group_check=True)
                pe.matmul(bank[2][:, 24:32], ones[:], nlf[:, 0, :], start=False, stop=False, skip_group_check=True)
                pe.matmul(bank[2][:, 24:32], upto[:, 0:P], nlf[:, 1, :], start=False, stop=True,
                          skip_group_check=True).then_inc(cum_done, 1)

            def fox_scores(h):
                s = bank[2 + h % 2]
                if h >= 2:
                    pe.wait_ge(shift_ready, h - 1)
                minus_f = [nlf[:, n, h:h + 1].broadcast_to([P, P]) for n in range(2)]
                kk = k_fox[:, h // 2, :]
                mm = lambda *a, **k: pe.matmul(*a, **k, skip_group_check=True)
                mm(s[:, 0:P], q_pad[:, h, 0:P], kk[:, 0:P], start=True, stop=False)
                mm(s[:, 0:P], minus_f[0], upto[:, 0:P], start=False, stop=True)
                mm(s[:, P:3 * P], q_pad[:, h, P:T], kk, start=False, stop=False)
                mm(s[:, P:3 * P], minus_f[0], upto[:], start=False, stop=False)
                mm(s[:, 2 * P:3 * P], minus_f[1], upto[:, 0:P], start=False, stop=True).then_inc(score_done, 1)

            def fox_turn(h):
                pe.wait_ge(p_ready, h + 1)
                if h >= 2:
                    pe.wait_ge(pt_ready, h - 1)
                for n in range(3):
                    ins = pe.transpose(bank[4 + h % 2][:, n * P:(n + 1) * P], prob[:, h % 2, n * P:(n + 1) * P], ident[:])
                ins.then_inc(turn_done, 1)

            def stick_scores(h):
                z = bank[2 + h % 2]
                if h < 2:
                    pe.wait_ge(shift_ready, 7 + h)
                else:
                    pe.wait_ge(lb_ready, h - 1)
                q = q_sb[:, h // 2, :]
                pe.matmul(z[:, 0:T], k_pad[:, h, 0:P], q, start=True, stop=True)
                pe.matmul(z[:, T:3 * P], k_pad[:, h, P:T], q[:, P:T], start=True, stop=True).then_inc(score_done, 1)

            def stick_sums(h):
                a = bank[4 + h % 2]
                m = sb_m[:, h % 2, :]
                pe.wait_ge(t_ready, h + 1)
                if h < 2:
                    pe.wait_ge(pt_ready, 7 + h)
                else:
                    pe.wait_ge(w_ready, h - 1)
                pe.matmul(a[:, 0:T], later[:], m[:, 0:T], start=True, stop=False, skip_group_check=True)
                pe.matmul(a[:, P:T], minus[:], m[:, T:3 * P], start=False, stop=True, skip_group_check=True)
                pe.matmul(a[:, T:3 * P], later[:], m[:, T:3 * P], start=False, stop=True,
                          skip_group_check=True).then_inc(turn_done, 1)

            def weighted_values(h):
                pe.wait_ge(pt_ready, h + 1)
                if h == 8:
                    pe.wait_ge(o_fox, 1)
                d = slice(64 * (h % 8), 64 * (h % 8) + 64)
                v = [v_tok[:, n, 64 * h:64 * h + 64] for n in range(2)]
                p = prob_t[:, h % 2, :] if h < 8 else sb_b[:, h % 2, :]
                pe.matmul(bank[6][:, d], p[:, 0:P], v[0], start=True, stop=True)
                pe.matmul(bank[7][:, d], p[:, P:T], v[0], start=True, stop=False)
                pe.matmul(bank[7][:, d], p[:, T:3 * P], v[1], start=False, stop=True).then_inc(pv_done, 1)

            def attend(s):
                if s < 8:
                    fox_scores(s)
                elif s < 16:
                    stick_scores(s - 8)
                if 1 <= s <= 8:
                    fox_turn(s - 1)
                elif 9 <= s <= 16:
                    stick_sums(s - 9)
                if s >= 2:
                    weighted_values(s - 2)

            for c in range(12):
                bank_free(c)
                if c == 6:
                    pe.wait_ge(pad_zero, 4)
                    pe.wait_ge(cum_ready, 1)
                for h in range(2):
                    half_chunk(c, h, bank[c % 2], act_hi, act_lo, ready=operand(0) if c == 0 else None,
                               moving=order1[c][0][1] == "v")
                    if c == 6 and h == 0:
                        pe.wait_ge(proj_free, 6)
                    if c >= 8 and c % 2 == 0 and h == 0:
                        pe.wait_ge(proj_free, c)
                    if c >= 6:
                        attend(2 * (c - 6) + h)
                if c == 0:
                    forget_logits()
                if c == 2:
                    forget_sums()
            pe.wait_ge(proj_free, 12)
            for s in range(12, 18):
                attend(s)
            for j in range(4):
                for n in range(4):
                    k, t = 2 * j + n // 2, n % 2
                    if n % 2 == 0:
                        pe.wait_ge(on_ready, 2 * (k // 4) + 2)
                    ins = pe.transpose(bank[2 + j][:, n * P:(n + 1) * P], o_tok[:, t, k * P:(k + 1) * P], ident[:])
                ins.then_inc(ot_turned, 1)
            for n in range(4):
                bank_free(OUT1 + n)
                chunk(OUT1 + n, bank[proj(OUT1 + n) % 2], act_hi, act_lo,
                      ready=(lambda k: pe.wait_ge(ot1_lo, k // 2 + 1) if k % 2 == 0 else None) if n == 0 else None)
            square_sums(1)
            gated_layer(UP1, 0, 1, 1)
            down_layer(DOWN1, 0)
            mod_sums(0)
            square_sums(2)
            square_sums(3)

            def head_sums(n):
                pe.wait_ge(qk_sq, n + 1)
                if n:
                    pe.wait_ge(qk_a, n)
                pe.matmul(bank[7][:], ones[:], h_sq[:], start=True, stop=True).then_inc(qk_ss, 1)

            def attend2(s):
                if s < 8:
                    b = bank[2 + s % 2]
                    pe.wait_ge(qk_norm, 2 * (s // 2) + 2)
                    if s >= 2:
                        pe.wait_ge(m2_ready, s - 1)
                    pe.matmul(b[:, 0:P], q2[:, s, 0:P], k2[:, s, 0:P], start=True, stop=True)
                    pe.matmul(b[:, P:3 * P], q2[:, s, P:T], k2[:, s, :], start=True, stop=True).then_inc(s2_done, 1)
                if 1 <= s <= 8:
                    h = s - 1
                    pe.wait_ge(p2_ready, h + 1)
                    if h:
                        pe.wait_ge(pt2_ready, h)
                    for n in range(3):
                        ins = pe.transpose(bank[4][:, n * P:(n + 1) * P], prob2[:, h % 2, n * P:(n + 1) * P], ident[:])
                    ins.then_inc(t2_done, 1)
                if s >= 2:
                    h = s - 2
                    pe.wait_ge(pt2_ready, h + 1)
                    if h >= 2:
                        pe.wait_ge(o2_lo, h - 1)
                    o = bank[5 + h % 2]
                    v = [v2[:, n, P * h:P * h + P] for n in range(2)]
                    pt = prob2_t[:, h % 2, :]
                    pe.matmul(o[:, 0:T], v[0], pt[:, 0:T], start=True, stop=False, skip_group_check=True)
                    pe.matmul(o[:, P:T], v[1], pt[:, T:3 * P], start=False, stop=True,
                              skip_group_check=True).then_inc(pv2_done, 1)

            for c in range(12):
                bank_free(QKV + c)
                for h in range(2):
                    half_chunk(QKV + c, h, bank[c % 2], act_hi, act_lo, ready=operand(2) if c == 0 else None,
                               moving=order2[c][0] == "v")
                    if h == 0 and c >= 5:
                        head_sums(c - 5)
                if c >= 6:
                    attend2(c - 6)
            head_sums(7)
            for s in range(6, 10):
                attend2(s)
            for n in range(4):
                bank_free(OUT2 + n)
                chunk(OUT2 + n, bank[proj(OUT2 + n) % 2], ot_hi, ot_lo,
                      ready=(lambda k: pe.wait_ge(o2_lo, k + 1)) if n == 0 else None)
            square_sums(4)
            gated_layer(UP2, PAIRS, 3, 3)
            down_layer(DOWN2, PAIRS)
            mod_sums(1)
            square_sums(5)

            for c in range(12):
                bank_free(IN3 + c)
                chunk(IN3 + c, bank[c % 2], act_hi, act_lo, ready=operand(4) if c == 0 else None)
            for n in range(4):
                bank_free(OUT3 + n)
                chunk(OUT3 + n, bank[proj(OUT3 + n) % 2], ot_hi, ot_lo,
                      ready=(lambda k: pe.wait_ge(sc_lo, k // 2 + 1) if k % 2 == 0 else None) if n == 0 else None)
            square_sums(6)
            gated_layer(UP3, 2 * PAIRS, 1, 5)
            down_layer(DOWN3, 2 * PAIRS)
            for t in range(2):
                for g in range(2):
                    for n in range(4):
                        k = 4 * g + n
                        if n % 2 == 0:
                            pe.wait_ge(res_ready, 4 * 7 + k // 2 + 1)
                        ins = pe.transpose(bank[2 * t + g][:, n * P:(n + 1) * P], res[:, k, t * P:(t + 1) * P], ident[:])
                    ins.then_inc(out_turned, 1)


INPUTS = ["x", "attn_norm_g", "w_in", "forget_bias", "fox_out_g", "sb_out_g", "w_out", "ffn_norm_g", "w_up", "conv_w",
          "conv_b", "w_down", "final_norm_g", "c_2", "w_ada_2", "b_ada_2", "norm_mix_2", "norm_ffn_2", "w_qkv_2",
          "w_o_2", "q_gain_2", "k_gain_2", "w_in_2", "conv_w_2", "w_out_2", "w_gate_up_2", "w_down_2"]


def kernel(**inputs):
    import numpy as np
    import concourse.bacc as bacc
    from concourse.bass_utils import run_bass_kernel_spmd

    nc = bacc.Bacc("TRN2", target_bir_lowering=False, num_devices=1)
    arrays, args = {}, []
    for name in INPUTS:
        a = np.ascontiguousarray(inputs[name])
        arrays[f"in_{name}"] = a
        args.append(nc.dram_tensor(f"in_{name}", a.shape, mybir.dt.from_np(a.dtype), kind="ExternalInput").ap())
    args.append(nc.dram_tensor("out", (1, T, D), F32, kind="ExternalOutput").ap())
    model_kernel(nc, *args)
    return run_bass_kernel_spmd(nc, [arrays], core_ids=[0]).results[0]["out"]
```

```python
from contextlib import ExitStack

import concourse.bass as bass
from concourse import mybir

F32 = mybir.dt.float32
F32R = mybir.dt.float32r
ACT = mybir.ActivationFunctionType
ALU = mybir.AluOpType
AX = mybir.AxisListType

P = 128
T = 256
D = 1024
KT = D // P
FF = 2816
FT = FF // P
CW = 256
UNIT = 4 * CW
EPS = 1e-6
LOG_EXP_SET, SILU_SET = "natural_log_exp_and_others", "silu_and_others"
NEG = -1e30

IN1, OUT1, UP1, DOWN1 = 0, 12, 16, 38
QKV, OUT2, UP2, DOWN2 = 49, 61, 65, 87
IN3, OUT3, UP3, DOWN3, CHUNKS = 98, 110, 114, 136, 147
RAW = 4
SPLIT = 4
PAIRS = FF // CW
ADA = 24
ADA_W = 2048

V_ATTN, V_FOX, V_SB, V_FFN, V_FINAL, V_MIX2, V_FFN2 = 0, 8, 12, 16, 24, 32, 48
V_QG, V_KG, V_CONV2, V_C, V_ROWS0 = 64, 65, 66, 90, 98
V_TAP = {0: (1, 0), 1: (1, 44), 2: (2, 0)}
V_CONVB = (2, 44)
V_BANKS, X_BANKS = (4, 5, 6, 2), (0, 1, 3, 7)
ROWS = (V_ROWS0, 88, 88, 96)
SUM_BANK = (2, 6, 2, 2, 6, 2, 6)
STEPS1 = {(2, 0): (0,), (2, 1): (1,), (3, 0): (2,), (3, 1): (3,), (5, 0): (4,), (5, 1): (5,), (6, 0): (6,), (6, 1): (7,),
          (8, 0): (8,), (8, 1): (9,), (9, 0): (10,), (9, 1): (11,), (11, 0): (12,), (11, 1): (13,), (12, 0): (14,),
          (12, 1): (15,), (13, 0): (16,), (13, 1): (17,)}
STEPS2 = {(3, 0): (0,), (4, 0): (1,), (5, 0): (2,), (6, 0): (3,), (8, 0): (4,), (9, 0): (5,), (11, 0): (6,), (11, 1): (7,),
          (12, 1): (8,), (13, 1): (9,)}
QK_AT, V_AT = (0, 1, 2, 3, 5, 6, 8, 9), (4, 7, 10, 11)
SH_M, SC_M, G_M, SH_F, SC_F, G_F = (KT * n for n in range(6))
PIECES = ((0, 0, 15), (0, 16, 31), (0, 32, 47), (1, 0, 15), (1, 16, 31), (1, 32, 39), (1, 40, 47))


def at(const, step, i):
    return const if i is None else i * step + const


def after(plan, c, h):
    return plan.get((c, h), ())


def cols(const, step, i, size):
    return slice(const, const + size) if i is None else bass.ds(i * step + const, size)


def model_kernel(nc, x, attn_norm_g, w_in, forget_bias, fox_out_g, sb_out_g, w_out, ffn_norm_g, w_up,
                 conv_w, conv_b, w_down, final_norm_g, c_2, w_ada_2, b_ada_2, norm_mix_2, norm_ffn_2,
                 w_qkv_2, w_o_2, q_gain_2, k_gain_2, w_in_2, conv_w_2, w_out_2, w_gate_up_2, w_down_2, out):
    ctx = ExitStack()
    with ctx:
        def sb(name, shape, dt=F32, stack=ctx):
            return stack.enter_context(nc.sbuf_tensor(name, shape, dt))

        def sem(name):
            return ctx.enter_context(nc.semaphore(name))

        w_raw = sb("w_raw", [P, RAW, 2 * UNIT])
        w_hi = sb("w_hi", [P, SPLIT, UNIT], F32R)
        w_lo = sb("w_lo", [P, SPLIT, UNIT], F32R)
        res = sb("res", [P, KT, T])
        act_hi = sb("act_hi", [P, KT, T], F32R)
        act_lo = sb("act_lo", [P, KT, T], F32R)
        ada_raw = sb("ada_raw", [P, 2, ADA_W])
        ada_acc = sb("ada_acc", [P, 3, ADA_W])
        vec = sb("vec", [P, 4, P])
        mod = sb("mod", [P, 2, 6 * KT])
        gain2 = sb("gain2", [P, 4, KT])
        silu_c = sb("silu_c", [P, KT])
        qk_gain = sb("qk_gain", [P, 1])
        q_rms = sb("q_rms", [P, 3, 4])
        q_rstd = sb("q_rstd", [P, 4, 4])
        ident = sb("ident", [P, P])
        ones = sb("ones", [P, P])
        upto = sb("upto", [P, T])
        causal = sb("causal", [P, T])
        later = sb("later", [P, P])
        minus = sb("minus", [P, P])
        before = sb("before", [P, 3 * P])
        rowsum = sb("rowsum", [P, 16, 2])
        nmax = sb("nmax", [P, 16, 2])
        rinv = sb("rinv", [P, 16, 2])
        small = sb("small", [P, 4, 8])
        wf_raw = sb("wf_raw", [P, KT, 8])
        wf_hi = sb("wf_hi", [P, KT, 8], F32R)
        wf_lo = sb("wf_lo", [P, KT, 8], F32R)
        fbias = sb("fbias", [P, 8])
        f_abs = sb("f_abs", [P, 2, 8])
        f_log = sb("f_log", [P, 2, 8])
        f_neg = sb("f_neg", [P, 2, 8])
        nlf = sb("nlf", [P, 2, 8])
        f_cum = sb("f_cum", [P, 2, 8])

        phase = ExitStack()
        scr = sb("scr", [P, KT, T], stack=phase)
        n_a = sb("n_a", [P, T], stack=phase)
        n_y = sb("n_y", [P, T], stack=phase)
        n_t = sb("n_t", [P, T], stack=phase)
        rstd = sb("rstd", [P, T], stack=phase)
        x_in = sb("x_in", [P, 2, D], stack=phase)
        v_in = sb("v_in", [P, 4, P], stack=phase)
        o_sb = sb("o_sb", [P, 2, D], stack=phase)
        phase.close()
        phase = ExitStack()
        q_pad = sb("q_pad", [P, 8, T], stack=phase)
        k_fox = sb("k_fox", [P, 4, T], stack=phase)
        k_pad = sb("k_pad", [P, 8, T], stack=phase)
        q_sb = sb("q_sb", [P, 4, T], stack=phase)
        v_tok = sb("v_tok", [P, 2, D], stack=phase)
        o_tok = sb("o_tok", [P, 2, D], stack=phase)
        logit = sb("logit", [P, 2, 3 * P], stack=phase)
        prob = sb("prob", [P, 2, 3 * P], stack=phase)
        prob_t = sb("prob_t", [P, 2, 3 * P], stack=phase)
        sb_l = sb("sb_l", [P, 2, 3 * P], stack=phase)
        sb_t = sb("sb_t", [P, 3 * P], stack=phase)
        sb_m = sb("sb_m", [P, 2, 3 * P], stack=phase)
        sb_b = sb("sb_b", [P, 2, 3 * P], stack=phase)
        fox_hi = sb("fox_hi", [P, 4, T], F32R, stack=phase)
        fox_lo = sb("fox_lo", [P, 4, T], F32R, stack=phase)
        phase.close()
        phase = ExitStack()
        hid_hi = sb("hid_hi", [P, FT, T], F32R, stack=phase)
        hid_lo = sb("hid_lo", [P, FT, T], F32R, stack=phase)
        conv = sb("conv", [P, 4, T], stack=phase)
        gated = sb("gated", [P, 2, T], stack=phase)
        hidden = sb("hidden", [P, 2, T], stack=phase)
        phase.close()
        phase = ExitStack()
        ot_hi = sb("ot_hi", [P, KT, T], F32R, stack=phase)
        ot_lo = sb("ot_lo", [P, KT, T], F32R, stack=phase)
        q2 = sb("q2", [P, KT, T], stack=phase)
        k2 = sb("k2", [P, KT, T], stack=phase)
        v2 = sb("v2", [P, 2, D], stack=phase)
        logit2 = sb("logit2", [P, 2, 3 * P], stack=phase)
        prob2 = sb("prob2", [P, 2, 3 * P], stack=phase)
        prob2_t = sb("prob2_t", [P, 2, 3 * P], stack=phase)
        h_sq = sb("h_sq", [P, 2 * T], stack=phase)
        h_a = sb("h_a", [P, 2 * T], stack=phase)
        h_y = sb("h_y", [P, 2 * T], stack=phase)
        h_t = sb("h_t", [P, 2 * T], stack=phase)
        phase.close()
        cgate, short, bprod = q2[:, 0:2, :], q2[:, 2:4, :], q2[:, 4:6, :]
        cu = q2[:, 6:8, :]

        bank = [ctx.enter_context(nc.psum_tensor(f"bank{n}", [P, 512], F32)) for n in range(8)]

        w_landed = [sem(f"w_landed{n}") for n in range(RAW)]
        hi_ready = sem("hi_ready")
        lo_ready = sem("lo_ready")
        unit_done = sem("unit_done")
        proj_free = sem("proj_free")
        ada_landed = [sem(f"ada_landed{n}") for n in range(2)]
        ada_used = sem("ada_used")
        ada_zero = sem("ada_zero")
        ada_red = sem("ada_red")
        mod_done = sem("mod_done")
        x_landed = sem("x_landed")
        v_landed = sem("v_landed")
        f_landed = sem("f_landed")
        fb_zero = sem("fb_zero")
        consts = sem("consts")
        x_turned = sem("x_turned")
        v_turned = sem("v_turned")
        vec_ready = sem("vec_ready")
        res_ready = sem("res_ready")
        sq_ready = sem("sq_ready")
        ss_ready = sem("ss_ready")
        na_ready = sem("na_ready")
        ln_ready = sem("ln_ready")
        y_ready = sem("y_ready")
        hx_ready = sem("hx_ready")
        h_hi = sem("h_hi")
        h_lo = sem("h_lo")
        wf_ready = sem("wf_ready")
        f_done = sem("f_done")
        f_act = sem("f_act")
        nlf_ready = sem("nlf_ready")
        cum_done = sem("cum_done")
        cum_ready = sem("cum_ready")
        v_ready = sem("v_ready")
        qk_ready = sem("qk_ready")
        score_done = sem("score_done")
        shift_ready = sem("shift_ready")
        p_ready = sem("p_ready")
        turn_done = sem("turn_done")
        pt_ready = sem("pt_ready")
        pv_done = sem("pv_done")
        z_ln = sem("z_ln")
        t_ready = sem("t_ready")
        lb_ready = sem("lb_ready")
        w_ready = sem("w_ready")
        a_ready = sem("a_ready")
        pad_zero = sem("pad_zero")
        o_fox = sem("o_fox")
        o_ready = sem("o_ready")
        oss_ready = sem("oss_ready")
        oms_ready = sem("oms_ready")
        oln = sem("oln")
        oy = sem("oy")
        on_ready = sem("on_ready")
        ot_turned = sem("ot_turned")
        ot1_hi = sem("ot1_hi")
        ot1_lo = sem("ot1_lo")
        cv_lin = sem("cv_lin")
        tap1 = sem("tap1")
        gate_conv = sem("gate_conv")
        val_conv = sem("val_conv")
        sil_ready = sem("sil_ready")
        prod_ready = sem("prod_ready")
        hid_hi_r = sem("hid_hi_r")
        hid_lo_r = sem("hid_lo_r")
        qk_sq = sem("qk_sq")
        qk_ss = sem("qk_ss")
        qk_a = sem("qk_a")
        qk_ln = sem("qk_ln")
        qk_y = sem("qk_y")
        qk_norm = sem("qk_norm")
        v2_ready = sem("v2_ready")
        s2_done = sem("s2_done")
        m2_ready = sem("m2_ready")
        e2_ready = sem("e2_ready")
        p2_ready = sem("p2_ready")
        t2_done = sem("t2_done")
        pt2_ready = sem("pt2_ready")
        pv2_done = sem("pv2_done")
        o2_hi = sem("o2_hi")
        o2_lo = sem("o2_lo")
        cu_ready = sem("cu_ready")
        sc_lin = sem("sc_lin")
        sc_tap = sem("sc_tap")
        sc_out = sem("sc_out")
        sc_hi = sem("sc_hi")
        sc_lo = sem("sc_lo")
        dve_seq = sem("dve_seq")
        silu_r = sem("silu_r")
        out_turned = sem("out_turned")
        out_ready = [sem(f"out_ready{t}") for t in range(2)]
        stored = sem("stored")

        def unit(buf, u):
            return buf[:, u % SPLIT, :]

        def raw_half(c, h):
            return w_raw[:, c % RAW, h * UNIT:(h + 1) * UNIT]

        def vcol(tile, n, step=0, i=None):
            return vec[:, tile, cols(n, step, i, 1)]

        order1 = [(kind, base + CW * g) for q, k, v in ((("fq", 0), ("fk", 512), ("fv", 1024)),
                                                        (("sq", 1544), ("sk", 2056), ("sv", 2568)))
                  for g in range(2) for kind, base in (q, k, v)]
        order2 = [None] * 12
        for n, c in enumerate(QK_AT):
            order2[c] = (("k", D), ("q", 0))[n % 2][0], (D, 0)[n % 2] + CW * (n // 2)
        for n, c in enumerate(V_AT):
            order2[c] = "v", 2 * D + CW * n
        order3 = [(kind, base + CW * g) for g in range(4) for kind, base in (("c", D), ("u", 2 * D), ("b", 0))]

        def rows(a, k=None):
            a = a if k is None else a[:, k, :]
            return a.rearrange("a (k p) -> (a k) p", p=P)

        vectors = [(0, V_ATTN, rows(attn_norm_g)), (0, V_FOX, rows(fox_out_g)), (0, V_SB, rows(sb_out_g)),
                   (0, V_FFN, rows(ffn_norm_g)), (0, V_FINAL, final_norm_g.rearrange("(k p) -> k p", p=P)),
                   (0, V_MIX2, rows(norm_mix_2)), (0, V_FFN2, rows(norm_ffn_2)), (0, V_QG, q_gain_2),
                   (0, V_KG, k_gain_2), (0, V_C, rows(c_2)), (3, 0, rows(b_ada_2)),
                   (V_CONVB[0], V_CONVB[1], rows(conv_b))]
        vectors += [(0, V_CONV2 + KT * k, rows(conv_w_2, k)) for k in range(3)]
        vectors += [(*V_TAP[k], rows(conv_w, k)) for k in range(3)]

        block = ctx.enter_context(nc.Block())

        @block.sync
        def _(sp):
            def wide(w):
                return w.rearrange("(k p) n -> p k n", p=P)

            def load(c, src, i=None):
                if c >= RAW:
                    sp.wait_ge(lo_ready, at(2 * (c - RAW) + 2, 8, i))
                dst = w_raw[:, c % RAW, :].rearrange("p (k n) -> p k n", n=src.shape[2])
                sp.dma_start(dst, src).then_inc(w_landed[c % RAW], 16)

            def load_gated(c0, w, straight):
                def pair(c, p, i):
                    for n in range(2):
                        load(c + n, w[:, :, cols(n * FF + CW * p, 2 * CW, i, CW)], i)
                for p in range(straight):
                    pair(c0 + 2 * p, p, None)
                with sp.Fori(0, (PAIRS - straight) // 2) as i:
                    for j in range(2):
                        pair(c0 + 2 * (straight + j), straight + j, i)

            def load_out(c0, w):
                for n in range(4):
                    load(c0 + n, w[:, 4 * (n // 2):4 * (n // 2) + 4, n % 2 * 2 * CW:(n % 2 + 1) * 2 * CW])

            def load_down(c0, w):
                for d in range(3):
                    load(c0 + d, w[:, 2 * d:2 * d + 2, :])
                with sp.Fori(0, 2) as i:
                    for j in range(4):
                        load(c0 + 3 + j, w[:, cols(6 + 2 * j, 8, i, 2), :], i)

            for t in range(2):
                sp.dma_start(x_in[:, t, :], x[0, t * P:(t + 1) * P, :]).then_inc(x_landed, 16)
            w = wide(w_in[0])
            for n, (_, col) in enumerate(order1):
                load(IN1 + n, w[:, :, col:col + CW])
            load_out(OUT1, wide(w_out[0]))
            load_gated(UP1, wide(w_up[0]), 1)
            load_down(DOWN1, wide(w_down[0]))
            w = wide(w_qkv_2[0])
            for n, (_, col) in enumerate(order2):
                load(QKV + n, w[:, :, col:col + CW])
            load_out(OUT2, wide(w_o_2[0]))
            load_gated(UP2, wide(w_gate_up_2[0]), 3)
            load_down(DOWN2, wide(w_down_2[0]))
            w = wide(w_in_2[0])
            for n, (_, col) in enumerate(order3):
                load(IN3 + n, w[:, :, col:col + CW])
            load_out(OUT3, wide(w_out_2[0]))
            load_gated(UP3, wide(w_gate_up_2[1]), 1)
            load_down(DOWN3, wide(w_down_2[1]))
            for t in range(2):
                sp.wait_ge(out_ready[t], 2)
                sp.dma_start(out[0, t * P:(t + 1) * P, :], o_sb[:, t, :]).then_inc(stored, 16)
            sp.wait_ge(stored, 32)

        @block.gpsimd
        def _(pool):
            pool.memset(fbias[:], 0.0).then_inc(fb_zero, 1)
            pool.memset(ident[:], 0.0).then_inc(consts, 1)
            pool.memset(ones[:], 1.0).then_inc(consts, 1)
            pool.memset(upto[:], 1.0).then_inc(consts, 1)
            pool.memset(causal[:], 0.0).then_inc(consts, 1)
            pool.memset(later[:], -1.0).then_inc(consts, 1)
            pool.memset(minus[:], -1.0).then_inc(consts, 1)
            pool.memset(before[:], 1.0).then_inc(consts, 1)
            pool.wait_ge(consts, 7)
            pool.affine_select(ident[:], ident[:], [[-1, P]], ALU.not_equal, 1.0, base=0,
                               channel_multiplier=1).then_inc(consts, 1)
            pool.wait_ge(fb_zero, 1)
            pool.dma_start(fbias[0:1, :], forget_bias).then_inc(f_landed, 16)
            pool.dma_start(wf_raw[:], w_in[0].rearrange("(k p) n -> p k n", p=P)[:, :, 1536:1544]).then_inc(f_landed, 16)
            pool.affine_select(upto[:], upto[:], [[1, T]], ALU.is_ge, 0.0, base=0,
                               channel_multiplier=-1).then_inc(consts, 1)
            pool.affine_select(causal[:], causal[:], [[-1, T]], ALU.is_ge, NEG, base=P,
                               channel_multiplier=1).then_inc(consts, 1)
            pool.affine_select(later[:], later[:], [[-1, P]], ALU.is_gt, 0.0, base=0,
                               channel_multiplier=1).then_inc(consts, 1)
            for lo, n in ((0, T), (T, P)):
                pool.affine_select(before[:, lo:lo + n], before[:, lo:lo + n], [[1, n]], ALU.is_gt, 0.0, base=0,
                                   channel_multiplier=-1).then_inc(consts, 1)
            for l in range(2):
                if l == 0:
                    for s in range(3):
                        pool.memset(ada_acc[:, s, :], 0.0).then_inc(ada_zero, 1)
                for s in range(3):
                    if l:
                        pool.wait_ge(ada_red, s + 1)
                        pool.memset(ada_acc[:, s, :], 0.0).then_inc(ada_zero, 1)
                    def fetch(i, j):
                        pool.dma_start(ada_raw[:, j, :], w_ada_2[l][cols(j * P, 2 * P, i, P), s * ADA_W:(s + 1) * ADA_W]
                                       ).then_inc(ada_landed[j], 16)
                    first = ADA * l + 8 * s
                    if first == 0:
                        fetch(None, 0)
                        fetch(None, 1)
                    with pool.Fori(int(first == 0), 4) as i:
                        for j in range(2):
                            pool.wait_ge(ada_used, at(first + j - 1, 2, i))
                            fetch(i, j)

        @block.scalar
        def _(act):
            def split(c, i=None):
                act.wait_ge(w_landed[c % RAW], at(16 * (c // RAW + 1), 16, i))
                for h in range(2):
                    split_unit(c, h, i)

            def split_unit(c, h, i=None):
                u = 2 * c + h
                if h == 0:
                    act.wait_ge(w_landed[c % RAW], at(16 * (c // RAW + 1), 16, i))
                if u >= SPLIT:
                    act.wait_ge(unit_done, at(u - SPLIT + 1, 8, i))
                act.activation(unit(w_hi, u), raw_half(c, h), ACT.Copy).then_inc(hi_ready, 1)

            def squares(n, version):
                for j in range(4):
                    act.wait_ge(res_ready, 4 * version + j + 1)
                    act.activation(scr[:, 2 * j:2 * j + 2, :], res[:, 2 * j:2 * j + 2, :],
                                   ACT.Square).then_inc(sq_ready, 1)

            def norm(n, m=None, shift=None, late=None):
                if late is not None:
                    split_unit(*late)
                act.wait_ge(na_ready, n + 1)
                act.activation(n_y[:], n_a[:], ACT.Ln, scale=-2.0).then_inc(ln_ready, 1)
                act.wait_ge(ln_ready, n + 1)
                act.activation(n_y[:], n_y[:], ACT.Exp, scale=-0.5).then_inc(y_ready, 1)
                if n in (1, 4, 6):
                    act.preload_act_table_set(SILU_SET)
                if m is None:
                    return
                for j in range(4):
                    act.wait_ge(hx_ready, 8 * m + 2 * j + 2)
                    if shift is None:
                        act.activation(act_hi[:, 2 * j:2 * j + 2, :], scr[:, 2 * j:2 * j + 2, :],
                                       ACT.Copy).then_inc(h_hi, 2)
                    else:
                        for k in (2 * j, 2 * j + 1):
                            act.activation(act_hi[:, k, :], scr[:, k, :], ACT.Identity,
                                           bias=shift(k)).then_inc(h_hi, 1)

            def gated_pair(c, pair, p, i, convolve):
                gate, val = bank[2 * (p % 2)], bank[2 * (p % 2) + 1]
                act.wait_ge(unit_done, at(2 * c + 4, 8, i))
                if convolve:
                    for q in range(4):
                        src = (gate, val)[q // 2][:, (q % 2) * T:(q % 2 + 1) * T]
                        f = (q // 2) * FT + 2 * p + q % 2
                        act.activation(conv[:, q, :], src, ACT.Identity, bias=vcol(2, 44 + f, 4, i),
                                       scale=vcol(2, f, 4, i)).then_inc(cv_lin, 1)
                    act.wait_ge(gate_conv, at(pair + 1, 2, i))
                    act.activation(gated[:], conv[:, 0:2, :], ACT.Silu).then_inc(sil_ready, 1)
                else:
                    act.activation(gated[:], gate[:].rearrange("p (t n) -> p t n", n=T), ACT.Silu
                                   ).then_inc(sil_ready, 1)
                act.wait_ge(prod_ready, at(pair + 1, 2, i))
                act.activation(hid_hi[:, cols(2 * p, 4, i, 2), :], hidden[:], ACT.Copy).then_inc(hid_hi_r, 1)

            def gated_layer(c0, pair0, straight, convolve):
                def step(c, pair, p, i):
                    split(c + 2, i)
                    split(c + 3, i)
                    gated_pair(c, pair, p, i, convolve)
                for p in range(straight):
                    step(c0 + 2 * p, pair0 + p, p, None)
                with act.Fori(0, (PAIRS - straight) // 2) as i:
                    for j in range(2):
                        p = straight + j
                        step(c0 + 2 * p, pair0 + p, p, i)

            def down_layer(c0):
                act.preload_act_table_set(LOG_EXP_SET)

                def rows(d, i=None):
                    if d:
                        split_unit(c0 + d + 1, 1, i)
                    split_unit(c0 + d + 2, 0, i)
                for d in range(3):
                    rows(d)
                if c0 == DOWN3:
                    for d in range(3, 9):
                        rows(d)
                    split_unit(c0 + 10, 1)
                    return
                with act.Fori(0, 2) as i:
                    for j in range(4):
                        rows(3 + j, i)

            for tile, row, src in vectors:
                act.dma_start(v_in[row:row + src.shape[0], tile, :], src).then_inc(v_landed, 16)
            act.wait_ge(vec_ready, 1)
            act.activation(silu_c[:], vec[:, 0, V_C:V_C + KT], ACT.Silu).then_inc(silu_r, 1)
            act.preload_act_table_set(LOG_EXP_SET)
            squares(0, 0)
            act.wait_ge(f_landed, 32)
            act.activation(wf_hi[:], wf_raw[:], ACT.Copy).then_inc(wf_ready, 1)
            norm(0, 0)
            split(0)
            split(1)

            def fox_exp(h):
                act.wait_ge(shift_ready, h + 1)
                for t, (lo, hi) in enumerate(((0, P), (P, 3 * P))):
                    ins = act.activation(prob[:, h % 2, lo:hi], logit[:, h % 2, lo:hi], ACT.Exp,
                                         bias=nmax[:, h, t:t + 1], accum_out=rowsum[:, h, t:t + 1])
                ins.then_inc(p_ready, 1)

            def fox_turned(h):
                act.wait_ge(turn_done, h + 1)
                if h >= 2:
                    act.wait_ge(pv_done, h - 1)
                act.activation(prob_t[:, h % 2, :], bank[4 + h % 2][:, 0:3 * P], ACT.Copy).then_inc(pt_ready, 1)

            def stick_logs(h):
                b = sb_l[:, h % 2, :]
                act.wait_ge(score_done, 8 + h + 1)
                if h >= 2:
                    act.wait_ge(t_ready, h - 1)
                act.activation(b, bank[2 + h % 2][:, 0:3 * P], ACT.Abs).then_inc(z_ln, 1)
                act.wait_ge(z_ln, 3 * h + 1)
                act.activation(b, b, ACT.Exp, scale=-1.0).then_inc(z_ln, 1)
                act.wait_ge(z_ln, 3 * h + 2)
                act.activation(b, b, ACT.Ln, bias=1.0).then_inc(z_ln, 1)

            def stick_weights(h):
                act.wait_ge(w_ready, h + 1)
                b = sb_b[:, h % 2, :]
                act.activation(b, b, ACT.Exp).then_inc(a_ready, 1)

            def attend(s):
                if 1 <= s <= 8:
                    fox_turned(s - 1)
                if s < 8:
                    fox_exp(s)
                elif s < 16:
                    stick_logs(s - 8)
                if 9 <= s <= 16:
                    stick_weights(s - 9)

            def forget():
                act.wait_ge(f_done, 1)
                act.activation(f_abs[:], bank[2][:, 0:16].rearrange("p (t n) -> p t n", n=8), ACT.Abs
                               ).then_inc(f_act, 1)
                act.wait_ge(f_act, 1)
                act.activation(f_log[:], f_abs[:], ACT.Exp, scale=-1.0).then_inc(f_act, 1)
                act.wait_ge(f_act, 2)
                act.activation(f_log[:], f_log[:], ACT.Ln, bias=1.0).then_inc(f_act, 1)

            def output_squares(g):
                act.wait_ge((o_fox, o_ready)[g], 1)
                for t in range(2):
                    ins = act.activation(q_pad[:, 4 * t + 2 * g:4 * t + 2 * g + 2, :].rearrange("p h n -> p (h n)"),
                                         o_tok[:, t, g * 512:(g + 1) * 512], ACT.Square,
                                         accum_out=small[:, g, t:t + 1])
                ins.then_inc(oss_ready, 1)

            def output_rms(g):
                act.wait_ge(oms_ready, g + 1)
                act.activation(small[:, g, 4:6], small[:, g, 2:4], ACT.Ln, scale=-2.0).then_inc(oln, 1)
                act.wait_ge(oln, g + 1)
                act.activation(small[:, g, 6:8], small[:, g, 4:6], ACT.Exp, scale=-0.5).then_inc(oy, 1)

            def output_hi(g):
                for j in (2 * g, 2 * g + 1):
                    act.wait_ge(ot_turned, j + 1)
                    for k in (2 * j, 2 * j + 1):
                        dst = fox_hi[:, k, :] if g == 0 else act_hi[:, k, :]
                        ins = act.activation(dst, bank[2 + j][:, (k % 2) * T:(k % 2 + 1) * T], ACT.Copy,
                                             scale=vcol(0, V_FOX + k))
                    ins.then_inc(ot1_hi, 1)

            for c in range(14):
                for h in range(2):
                    split_unit(c + 2, h)
                    if (c, h) == (0, 1):
                        forget()
                    if (c, h) == (10, 0):
                        output_hi(0)
                    for s in after(STEPS1, c, h):
                        attend(s)
                    if (c, h) == (9, 0):
                        output_squares(0)
                    if (c, h) == (9, 1):
                        output_rms(0)
            output_squares(1)
            output_rms(1)
            act.wait_ge(unit_done, 2 * OUT1)
            output_hi(1)
            split(OUT1 + 4)
            split_unit(OUT1 + 5, 0)
            squares(1, 1)
            norm(1, 1, late=(UP1 + 1, 1))
            gated_layer(UP1, 0, 1, True)
            down_layer(DOWN1)
            squares(2, 2)
            norm(2, late=(QKV + 1, 1))

            squares(3, 3)
            norm(3, 2, shift=lambda k: mod[:, 0, SH_M + k:SH_M + k + 1])

            def head_squares(n):
                act.wait_ge(unit_done, 2 * (QKV + QK_AT[n]) + 2)
                src = bank[QK_AT[n] % 2][:, :]
                if n:
                    act.wait_ge(qk_ss, n)
                act.activation(h_sq[:], src, ACT.Square)
                dst = (k2, q2)[n % 2][:, 2 * (n // 2):2 * (n // 2) + 2, :]
                act.activation(dst, src.rearrange("p (t n) -> p t n", n=T), ACT.Copy).then_inc(qk_sq, 1)

            def head_rms(n):
                a, y = (h_a[:], h_y[:]) if n % 2 == 0 else (q_rms[:, 0, :], q_rms[:, 1, :])
                act.wait_ge(qk_a, n + 1)
                act.activation(y, a, ACT.Ln, scale=-2.0).then_inc(qk_ln, 1)
                act.wait_ge(qk_ln, n + 1)
                act.activation(y, y, ACT.Exp, scale=-0.5).then_inc(qk_y, 1)

            def attend2(s):
                if s >= 2:
                    h = s - 2
                    act.wait_ge(pv2_done, h + 1)
                    act.activation(ot_hi[:, h, :], bank[5 + h % 2][:, 0:T], ACT.Copy).then_inc(o2_hi, 1)
                if 1 <= s <= 8:
                    h = s - 1
                    act.wait_ge(t2_done, h + 1)
                    if h >= 2:
                        act.wait_ge(pv2_done, h - 1)
                    act.activation(prob2_t[:, h % 2, :], bank[4][:, 0:3 * P], ACT.Copy).then_inc(pt2_ready, 1)
                if s < 8:
                    act.wait_ge(m2_ready, s + 1)
                    for t, (lo, hi) in enumerate(((0, P), (P, 3 * P))):
                        ins = act.activation(prob2[:, s % 2, lo:hi], logit2[:, s % 2, lo:hi], ACT.Exp,
                                             bias=nmax[:, s, t:t + 1], accum_out=rowsum[:, s, t:t + 1])
                    ins.then_inc(e2_ready, 1)

            for c in range(15):
                for h in range(2):
                    split_unit(QKV + c + 2, h)
                    if h == 0 and c - 1 in QK_AT:
                        head_rms(QK_AT.index(c - 1))
                    if h == 1 and c in QK_AT:
                        head_squares(QK_AT.index(c))
                    for s in after(STEPS2, c, h):
                        attend2(s)
            split_unit(UP2 + 1, 0)
            squares(4, 4)
            norm(4, 3, shift=lambda k: mod[:, 0, SH_F + k:SH_F + k + 1], late=(UP2 + 1, 1))
            gated_layer(UP2, PAIRS, 3, False)
            down_layer(DOWN2)

            squares(5, 5)
            norm(5, 4, shift=lambda k: mod[:, 1, SH_M + k:SH_M + k + 1], late=(IN3 + 1, 1))
            for c in range(12):
                split(IN3 + c + 2)
                g = c // 3
                if c % 3 == 1:
                    act.wait_ge(cu_ready, g + 1)
                    for t in range(2):
                        act.activation(short[:, t, :], cu[:, t, :], ACT.Identity, bias=0.0,
                                       scale=vcol(0, V_CONV2 + 2 * KT + 2 * g + t)).then_inc(sc_lin, 1)
                if c % 3 == 2:
                    act.wait_ge(sc_out, g + 1)
                    act.activation(ot_hi[:, 2 * g:2 * g + 2, :], bprod, ACT.Copy).then_inc(sc_hi, 1)
            for n in range(3):
                split(OUT3 + n + 2)
            split_unit(OUT3 + 5, 0)
            squares(6, 6)
            norm(6, 5, shift=lambda k: mod[:, 1, SH_F + k:SH_F + k + 1], late=(UP3 + 1, 1))
            gated_layer(UP3, 2 * PAIRS, 1, False)
            down_layer(DOWN3)
            for t in range(2):
                act.wait_ge(out_turned, 2 * t + 1)
                act.activation(o_sb[:, t, 0:512], bank[2 * t][:, :], ACT.Copy).then_inc(out_ready[t], 1)

        @block.vector
        def _(dve):
            seq = [0]

            def link(ins):
                seq[0] += 1
                ins.then_inc(dve_seq, 1)
                dve.wait_ge(dve_seq, seq[0])

            def split_unit(c, h, i=None):
                u = 2 * c + h
                dve.wait_ge(hi_ready, at(u + 1, 8, i))
                dve.tensor_tensor(unit(w_lo, u), raw_half(c, h), unit(w_hi, u).bitcast(F32),
                                  ALU.subtract).then_inc(lo_ready, 1)

            def split(c, i=None):
                for h in range(2):
                    split_unit(c, h, i)

            def ada(n, i=None):
                s, k = n % ADA // 8, n % 8
                if n % 8 == 0 or i is not None:
                    dve.wait_ge(ada_zero, 3 * (n // ADA) + s + 1)
                dve.wait_ge(ada_landed[n % 2], at(16 * (n // 2 + 1), 8 * ada_step[0], i))
                if n == 0:
                    dve.wait_ge(silu_r, 1)
                else:
                    dve.wait_ge(ada_used, at(n, ada_step[0], i))
                dve.scalar_tensor_tensor(ada_acc[:, s, :], ada_raw[:, n % 2, :], silu_c[:, cols(k, ada_step[0], i, 1)],
                                         ada_acc[:, s, :], ALU.mult, ALU.add).then_inc(ada_used, 1)
            ada_step = [4]

            def norm(n, gain, shift=None, version=None, late=None):
                dve.wait_ge(ss_ready, n + 1)
                dve.tensor_scalar(n_a[:], bank[SUM_BANK[n]][:, 0:T], -0.5 / D, -0.5 * EPS, ALU.mult,
                                  ALU.add).then_inc(na_ready, 1)
                if late is not None:
                    split_unit(*late)
                dve.wait_ge(y_ready, n + 1)
                link(dve.tensor_tensor(n_t[:], n_y[:], n_y[:], ALU.mult))
                link(dve.tensor_tensor(n_t[:], n_t[:], n_a[:], ALU.mult))
                link(dve.scalar_tensor_tensor(rstd[:], n_t[:], 1.5, n_y[:], ALU.add, ALU.mult))

                def part(k):
                    dst = scr if version is None else res
                    ins = dve.scalar_tensor_tensor(dst[:, k, :], res[:, k, :], gain(k), rstd[:], ALU.mult, ALU.mult)
                    if version is None:
                        ins.then_inc(hx_ready, 1)
                    elif k % 2:
                        ins.then_inc(res_ready, 1)

                def rest(j):
                    dve.wait_ge(h_hi, 8 * hn[0] + 2 * j + 2)
                    pair = slice(2 * j, 2 * j + 2)
                    if shift is None:
                        dve.tensor_tensor(act_lo[:, pair, :], scr[:, pair, :], act_hi[:, pair, :].bitcast(F32),
                                          ALU.subtract).then_inc(h_lo, 1)
                    else:
                        for k in (2 * j, 2 * j + 1):
                            ins = dve.scalar_tensor_tensor(act_lo[:, k, :], scr[:, k, :], shift(k),
                                                           act_hi[:, k, :].bitcast(F32), ALU.add, ALU.subtract)
                        ins.then_inc(h_lo, 1)
                for j in range(4):
                    part(2 * j)
                    part(2 * j + 1)
                    if version is None and j:
                        rest(j - 1)
                if version is None:
                    rest(3)
                    hn[0] += 1
            hn = [0]

            def add_up(c0, gate=None):
                for n in (2, 3):
                    split_unit(c0 + n + 2, 0)
                    if n == 2:
                        split_unit(c0 + n + 2, 1)
                    dve.wait_ge(unit_done, 2 * (c0 + n) + 2)
                    for j in (2 * n - 4, 2 * n - 3):
                        update(bank[j], j, gate)

            def update(src, j, gate):
                pair = slice(2 * j, 2 * j + 2)
                if gate is None:
                    link(dve.tensor_tensor(res[:, pair, :], src[:].rearrange("p (t n) -> p t n", n=T), res[:, pair, :],
                                           ALU.add))
                else:
                    for t in range(2):
                        k = 2 * j + t
                        ins = dve.scalar_tensor_tensor(res[:, k, :], src[:, t * T:(t + 1) * T], gate(k), res[:, k, :],
                                                       ALU.mult, ALU.add)
                    link(ins)
                dve.sem_inc(res_ready, 1)

            def gated_pair(c, pair, p, i, convolve):
                gate, val = bank[2 * (p % 2)], bank[2 * (p % 2) + 1]
                if convolve:
                    for half, (src, done) in enumerate(((gate, gate_conv), (val, val_conv))):
                        dve.wait_ge(cv_lin, at(4 * pair + 2 * half + 2, 8, i))
                        for tap in (1, 0):
                            lag = 2 - tap
                            for q in (2 * half, 2 * half + 1):
                                tile, base = V_TAP[tap]
                                f = half * FT + 2 * p + q % 2
                                if tap == 0:
                                    dve.wait_ge(tap1, at(4 * pair + q + 1, 8, i))
                                ins = dve.scalar_tensor_tensor(conv[:, q, lag:T], src[:, (q % 2) * T:(q % 2 + 1) * T - lag],
                                                               vcol(tile, base + f, 4, i), conv[:, q, lag:T],
                                                               ALU.mult, ALU.add)
                                if tap == 1:
                                    ins.then_inc(tap1, 1)
                        ins.then_inc(done, 1)
                    dve.wait_ge(val_conv, at(pair + 1, 2, i))
                    value = conv[:, 2:4, :]
                else:
                    value = val[:].rearrange("p (t n) -> p t n", n=T)
                dve.wait_ge(sil_ready, at(pair + 1, 2, i))
                if pair or i is not None:
                    dve.wait_ge(hid_lo_r, at(pair, 2, i))
                dve.tensor_tensor(hidden[:], value, gated[:], ALU.mult).then_inc(prod_ready, 1)
                dve.wait_ge(hid_hi_r, at(pair + 1, 2, i))
                kt = cols(2 * p, 4, i, 2)
                dve.tensor_tensor(hid_lo[:, kt, :], hidden[:], hid_hi[:, kt, :].bitcast(F32),
                                  ALU.subtract).then_inc(hid_lo_r, 1)

            def gated_layer(c0, pair0, straight, convolve, ada0=None):
                def step(c, pair, p, i, j=None):
                    split(c + 2, i)
                    split(c + 3, i)
                    if ada0 is not None and i is not None:
                        ada(ada0 + j, i)
                    gated_pair(c, pair, p, i, convolve)
                for p in range(straight):
                    step(c0 + 2 * p, pair0 + p, p, None)
                ada_step[0] = 2
                with dve.Fori(0, (PAIRS - straight) // 2) as i:
                    for j in range(2):
                        p = straight + j
                        step(c0 + 2 * p, pair0 + p, p, i, j)
                ada_step[0] = 4

            def down_layer(c0, ada0, gate):
                def rows(d, i=None):
                    if d:
                        split_unit(c0 + d + 1, 1, i)
                    split_unit(c0 + d + 2, 0, i)
                for d in range(3):
                    rows(d)
                if c0 == DOWN3:
                    for d in range(3, 9):
                        rows(d)
                    split_unit(c0 + 10, 1)
                else:
                    with dve.Fori(0, 2) as i:
                        for j in range(4):
                            ada(ada0 + j, i)
                            rows(3 + j, i)
                dve.wait_ge(unit_done, 2 * (c0 + 11))
                for j in range(4):
                    update(bank[4 + j], j, gate)

            def modulation(piece):
                l, first, last = PIECES[piece]
                dve.wait_ge(ada_red, piece + 1)
                link(dve.tensor_tensor(mod[:, l, first:last + 1], bank[7][:, first:last + 1],
                                       vec[:, 3, 6 * KT * l + first:6 * KT * l + last + 1], ALU.add))
                dve.sem_inc(mod_done, 1)
                for n, (sc, g) in enumerate(((SC_M, V_MIX2), (SC_F, V_FFN2))):
                    if first <= sc <= last:
                        link(dve.scalar_tensor_tensor(gain2[:, 2 * l + n, :], mod[:, l, sc:sc + KT], 1.0,
                                                      vec[:, 0, g + KT * l:g + KT * (l + 1)], ALU.add, ALU.mult))

            for n in range(4):
                dve.wait_ge(v_turned, n + 1)
                dve.tensor_copy(vec[:, n, 0:ROWS[n]], bank[V_BANKS[n]][:, 0:ROWS[n]]).then_inc(vec_ready, 1)
            for j in range(4):
                dve.wait_ge(x_turned, j + 1)
                dve.tensor_copy(res[:, 2 * j:2 * j + 2, :], bank[X_BANKS[j]][:].rearrange("p (t n) -> p t n", n=T)
                                ).then_inc(res_ready, 1)
            dve.wait_ge(vec_ready, 4)
            dve.tensor_scalar(qk_gain[:], vec[:, 0, V_QG:V_QG + 1], vec[:, 0, V_KG:V_KG + 1], float(P) ** -0.5,
                              ALU.mult, ALU.mult)
            dve.wait_ge(wf_ready, 1)
            dve.tensor_tensor(wf_lo[:], wf_raw[:], wf_hi[:].bitcast(F32), ALU.subtract).then_inc(wf_ready, 1)
            dve.wait_ge(res_ready, 4)
            norm(0, lambda k: vcol(0, V_ATTN + k))
            split(0)
            split(1)
            dve.wait_ge(h_lo, 4)
            for half in range(2):
                rows = slice(64 * (1 - half), 64 * (2 - half))
                dve.memset(q_pad[rows, half:8:2, :], 0.0).then_inc(pad_zero, 1)
                dve.memset(k_pad[rows, half:8:2, :], 0.0).then_inc(pad_zero, 1)

            def place(c):
                kind = order1[c][0]
                g = c // 3 % 2
                src = bank[c % 2][:].rearrange("p (t n) -> p t n", n=T)
                dve.wait_ge(unit_done, 2 * c + 2)
                if kind[1] == "v":
                    base = CW * (c // 3)
                    dve.tensor_copy(v_tok[:, :, base:base + CW], src).then_inc(proj_free, 1)
                elif kind == "fk":
                    dve.tensor_copy(k_fox[:, 2 * g:2 * g + 2, :], src).then_inc(proj_free, 1)
                elif kind == "sq":
                    dve.tensor_scalar(q_sb[:, 2 * g:2 * g + 2, :], src, 0.125, None, ALU.mult).then_inc(proj_free, 1)
                else:
                    pad, scale = (q_pad, 0.125) if kind == "fq" else (k_pad, 1.0)
                    if c in (0, 7):
                        dve.wait_ge(pad_zero, 4)
                    for half in range(2):
                        rows = slice(64 * half, 64 * half + 64)
                        ins = dve.tensor_scalar(pad[rows, 4 * g + half:4 * g + 4:2, :], src[rows], scale, None, ALU.mult)
                    ins.then_inc(proj_free, 1)

            def fox_shift(h):
                dve.wait_ge(score_done, h + 1)
                s = bank[2 + h % 2]
                if h == 0:
                    dve.wait_ge(consts, 13)
                if h >= 2:
                    dve.wait_ge(p_ready, h - 1)
                dve.scalar_tensor_tensor(logit[:, h % 2, 0:P], s[:, 0:P], f_cum[:, 0, h:h + 1], causal[:, P:T],
                                         ALU.add, ALU.add)
                link(dve.scalar_tensor_tensor(logit[:, h % 2, P:3 * P], s[:, P:3 * P], f_cum[:, 1, h:h + 1], causal[:],
                                              ALU.add, ALU.add))
                dve.tensor_reduce(nmax[:, h, 0:1], logit[:, h % 2, 0:P], AX.X, ALU.max, negate=True)
                dve.tensor_reduce(nmax[:, h, 1:2], logit[:, h % 2, P:3 * P], AX.X, ALU.max,
                                  negate=True).then_inc(shift_ready, 1)

            def stick_parts(h):
                z = bank[2 + h % 2][:, 0:3 * P]
                dve.wait_ge(z_ln, 3 * h + 3)
                link(dve.scalar_tensor_tensor(sb_t[:], z, 0.0, sb_l[:, h % 2, :], ALU.max, ALU.add))
                if h >= 2:
                    dve.wait_ge(turn_done, 8 + h - 1)
                dve.tensor_tensor(sb_m[:, h % 2, :], sb_t[:], before[:], ALU.mult).then_inc(t_ready, 1)
                if h >= 2:
                    dve.wait_ge(pv_done, 8 + h - 1)
                dve.tensor_tensor(sb_b[:, h % 2, :], z, sb_t[:], ALU.subtract).then_inc(lb_ready, 1)

            def stick_sum(h):
                dve.wait_ge(turn_done, 8 + h + 1)
                dve.wait_ge(lb_ready, h + 1)
                b = sb_b[:, h % 2, :]
                dve.tensor_tensor(b, bank[4 + h % 2][:, 0:3 * P], b, ALU.add).then_inc(w_ready, 1)

            def stick_mask(h):
                dve.wait_ge(a_ready, h + 1)
                b = sb_b[:, h % 2, :]
                dve.tensor_tensor(b, b, before[:], ALU.mult).then_inc(pt_ready, 1)

            def outputs(g):
                if g == 0:
                    dve.wait_ge(p_ready, 8)
                    link(dve.reciprocal(rinv[:, 0:8, :], rowsum[:, 0:8, :]))
                dve.wait_ge(pv_done, 8 * g + 8)
                for t in range(2):
                    dst = o_tok[:, t, 512 * g:512 * (g + 1)]
                    if g == 0:
                        ins = dve.tensor_tensor(dst.rearrange("p (h d) -> p h d", d=64),
                                                bank[6 + t][:].rearrange("p (h d) -> p h d", d=64),
                                                rinv[:, 0:8, t:t + 1].broadcast_to([P, 8, 64]), ALU.mult)
                    else:
                        ins = dve.tensor_copy(dst, bank[6 + t][:])
                ins.then_inc(o_fox if g == 0 else o_ready, 1)

            def attend(s):
                if s < 8:
                    fox_shift(s)
                if 9 <= s <= 16:
                    stick_sum(s - 9)
                if 8 <= s < 16:
                    stick_parts(s - 8)
                if 9 <= s <= 16:
                    stick_mask(s - 9)

            def output_mean(g):
                dve.wait_ge(oss_ready, g + 1)
                dve.tensor_scalar(small[:, g, 2:4], small[:, g, 0:2], -0.5 / 512, -0.5 * EPS, ALU.mult,
                                  ALU.add).then_inc(oms_ready, 1)

            def output_norm(g):
                dve.wait_ge(oy, g + 1)
                a, y, t4, r4 = small[:, g, 2:4], small[:, g, 6:8], small[:, 2 + g, 0:2], small[:, 2 + g, 2:4]
                link(dve.tensor_tensor(t4, y, y, ALU.mult))
                link(dve.tensor_tensor(t4, t4, a, ALU.mult))
                link(dve.scalar_tensor_tensor(r4, t4, 1.5, y, ALU.add, ALU.mult))
                for t in range(2):
                    o = o_tok[:, t, g * 512:(g + 1) * 512]
                    dve.tensor_scalar(o, o, r4[:, t:t + 1], None, ALU.mult).then_inc(on_ready, 1)

            def output_lo(g):
                for j in (2 * g, 2 * g + 1):
                    dve.wait_ge(ot1_hi, j + 1)
                    for k in (2 * j, 2 * j + 1):
                        hi, lo = (fox_hi, fox_lo) if g == 0 else (act_hi, act_lo)
                        ins = dve.scalar_tensor_tensor(lo[:, k, :], bank[2 + j][:, (k % 2) * T:(k % 2 + 1) * T],
                                                       vcol(0, V_FOX + k), hi[:, k, :].bitcast(F32), ALU.mult, ALU.subtract)
                    ins.then_inc(ot1_lo, 1)

            for c in range(14):
                for h in range(2):
                    split_unit(c + 2, h)
                    if (c, h) == (0, 1):
                        dve.wait_ge(f_act, 1)
                        link(dve.tensor_scalar(f_neg[:], bank[2][:, 0:16].rearrange("p (t n) -> p t n", n=8), -1.0, 0.0,
                                               ALU.mult, ALU.max))
                        dve.wait_ge(f_act, 3)
                        dve.tensor_tensor(nlf[:], f_neg[:], f_log[:], ALU.add).then_inc(nlf_ready, 1)
                    if (c, h) == (1, 0):
                        dve.wait_ge(cum_done, 1)
                        dve.tensor_scalar(f_cum[:], bank[2][:, 16:32].rearrange("p (t n) -> p t n", n=8), -1.0, None,
                                          ALU.mult).then_inc(cum_ready, 1)
                    if (c, h) == (9, 0):
                        outputs(0)
                    if (c, h) == (10, 0):
                        output_lo(0)
                    if h == 1 and c < 12:
                        place(c)
                    for s in after(STEPS1, c, h):
                        attend(s)
                    if h == 0:
                        ada(c)
                    if (c, h) == (9, 0):
                        output_mean(0)
                    if (c, h) == (9, 1):
                        output_norm(0)
            outputs(1)
            output_mean(1)
            output_norm(1)
            output_lo(1)
            ada(14)
            ada(15)
            add_up(OUT1)
            norm(1, lambda k: vcol(0, V_FFN + k), late=(UP1 + 1, 1))
            modulation(0)
            gated_layer(UP1, 0, 1, True)
            down_layer(DOWN1, 16, None)
            norm(2, lambda k: vcol(0, V_FINAL + k), version=3, late=(QKV + 1, 1))

            modulation(1)
            norm(3, lambda k: gain2[:, 0, k:k + 1], shift=lambda k: mod[:, 0, SH_M + k:SH_M + k + 1])
            modulation(2)

            def head_mean(n):
                dve.wait_ge(qk_ss, n + 1)
                a, src = (h_a[:], bank[7][:]) if n % 2 == 0 else (q_rms[:, 0, :], bank[7][:, 0:4])
                dve.tensor_scalar(a, src, -0.5 / P, -0.5 * EPS, ALU.mult, ALU.add).then_inc(qk_a, 1)

            def head_norm(n):
                dve.wait_ge(qk_y, n + 1)
                a, y, t = (h_a[:], h_y[:], h_t[:]) if n % 2 == 0 else (q_rms[:, 0, :], q_rms[:, 1, :], q_rms[:, 2, :])
                link(dve.tensor_tensor(t, y, y, ALU.mult))
                link(dve.tensor_tensor(t, t, a, ALU.mult))
                if n % 2:
                    link(dve.scalar_tensor_tensor(q_rstd[:, n // 2, :], t, 1.5, y, ALU.add, ALU.mult))
                    dve.sem_inc(qk_norm, 1)
                else:
                    link(dve.scalar_tensor_tensor(t, t, 1.5, y, ALU.add, ALU.mult))
                    dst = k2[:, 2 * (n // 2):2 * (n // 2) + 2, :]
                    dve.scalar_tensor_tensor(dst, dst, qk_gain[:], t.rearrange("p (t n) -> p t n", n=T),
                                             ALU.mult, ALU.mult).then_inc(qk_norm, 1)

            def attend2(s):
                if s >= 2:
                    h = s - 2
                    dve.wait_ge(o2_hi, h + 1)
                    dve.tensor_tensor(ot_lo[:, h, :], bank[5 + h % 2][:, 0:T], ot_hi[:, h, :].bitcast(F32),
                                      ALU.subtract).then_inc(o2_lo, 1)
                if s < 8:
                    dve.wait_ge(s2_done, s + 1)
                    b = bank[2 + s % 2]
                    rq = [q_rstd[:, s // 2, 2 * (s % 2) + t:2 * (s % 2) + t + 1] for t in range(2)]
                    dve.scalar_tensor_tensor(logit2[:, s % 2, 0:P], b[:, 0:P], rq[0], causal[:, P:T], ALU.mult, ALU.add)
                    link(dve.scalar_tensor_tensor(logit2[:, s % 2, P:3 * P], b[:, P:3 * P], rq[1], causal[:],
                                                  ALU.mult, ALU.add))
                    dve.tensor_reduce(nmax[:, s, 0:1], logit2[:, s % 2, 0:P], AX.X, ALU.max, negate=True)
                    dve.tensor_reduce(nmax[:, s, 1:2], logit2[:, s % 2, P:3 * P], AX.X, ALU.max,
                                      negate=True).then_inc(m2_ready, 1)

            def weights2(s):
                dve.wait_ge(e2_ready, s + 1)
                link(dve.reciprocal(rinv[:, s, :], rowsum[:, s, :]))
                for t, (lo, hi) in enumerate(((0, P), (P, 3 * P))):
                    ins = dve.tensor_scalar(prob2[:, s % 2, lo:hi], prob2[:, s % 2, lo:hi], rinv[:, s, t:t + 1], None,
                                            ALU.mult)
                ins.then_inc(p2_ready, 1)

            for c in range(14):
                for h in range(2):
                    split_unit(QKV + c + 2, h)
                    if h == 0 and c - 1 in QK_AT:
                        head_mean(QK_AT.index(c - 1))
                    if h == 1 and c in V_AT:
                        n = V_AT.index(c)
                        dve.wait_ge(unit_done, 2 * (QKV + c) + 2)
                        dve.tensor_copy(v2[:, :, CW * n:CW * (n + 1)], bank[c % 2][:].rearrange("p (t n) -> p t n", n=T)
                                        ).then_inc(v2_ready, 1)
                    for s in after(STEPS2, c, h):
                        attend2(s)
                    if h == 1 and c - 1 in QK_AT:
                        head_norm(QK_AT.index(c - 1))
                    if h == 0 and c in (0, 2, 5, 7, 8, 10, 12, 13):
                        ada(ADA + (0, 2, 5, 7, 8, 10, 12, 13).index(c))
                    for s in after(STEPS2, c, h):
                        if s < 8:
                            weights2(s)
            add_up(OUT2, lambda k: mod[:, 0, G_M + k:G_M + k + 1])
            norm(4, lambda k: gain2[:, 1, k:k + 1], shift=lambda k: mod[:, 0, SH_F + k:SH_F + k + 1], late=(UP2 + 1, 1))
            modulation(3)
            gated_layer(UP2, PAIRS, 3, False, ADA + 8)
            down_layer(DOWN2, ADA + 16, lambda k: mod[:, 0, G_F + k:G_F + k + 1])

            norm(5, lambda k: gain2[:, 2, k:k + 1], shift=lambda k: mod[:, 1, SH_M + k:SH_M + k + 1], late=(IN3 + 1, 1))
            modulation(4)
            for c in range(12):
                split(IN3 + c + 2)
                g = c // 3
                src = bank[c % 2][:].rearrange("p (t n) -> p t n", n=T)
                dve.wait_ge(unit_done, 2 * (IN3 + c) + 2)
                if c % 3 == 0:
                    link(dve.tensor_copy(cgate, src))
                    dve.sem_inc(proj_free, 1)
                elif c % 3 == 1:
                    dve.tensor_tensor(cu, src, cgate, ALU.mult).then_inc(cu_ready, 1)
                    dve.wait_ge(cu_ready, g + 1)
                    dve.sem_inc(proj_free, 1)
                    for tap in (1, 0):
                        lag = 2 - tap
                        for t in range(2):
                            if tap == 1:
                                dve.wait_ge(sc_lin, 2 * g + t + 1)
                            else:
                                dve.wait_ge(sc_tap, 4 * g + t + 1)
                            dve.scalar_tensor_tensor(short[:, t, lag:T], cu[:, t, 0:T - lag],
                                                     vcol(0, V_CONV2 + KT * tap + 2 * g + t), short[:, t, lag:T],
                                                     ALU.mult, ALU.add).then_inc(sc_tap, 1)
                else:
                    dve.wait_ge(sc_tap, 4 * g + 4)
                    dve.tensor_tensor(bprod, src, short, ALU.mult).then_inc(sc_out, 1)
                    dve.wait_ge(sc_out, g + 1)
                    dve.sem_inc(proj_free, 1)
                    dve.wait_ge(sc_hi, g + 1)
                    pair = slice(2 * g, 2 * g + 2)
                    dve.tensor_tensor(ot_lo[:, pair, :], bprod, ot_hi[:, pair, :].bitcast(F32),
                                      ALU.subtract).then_inc(sc_lo, 1)
            split(OUT3 + 2)
            split(OUT3 + 3)
            add_up(OUT3, lambda k: mod[:, 1, G_M + k:G_M + k + 1])
            modulation(5)
            norm(6, lambda k: gain2[:, 3, k:k + 1], shift=lambda k: mod[:, 1, SH_F + k:SH_F + k + 1], late=(UP3 + 1, 1))
            modulation(6)
            gated_layer(UP3, 2 * PAIRS, 1, False)
            down_layer(DOWN3, None, lambda k: mod[:, 1, G_F + k:G_F + k + 1])
            for t in range(2):
                dve.wait_ge(out_turned, 2 * t + 2)
                dve.tensor_copy(o_sb[:, t, 512:D], bank[2 * t + 1][:, :]).then_inc(out_ready[t], 1)

        @block.tensor
        def _(pe):
            def products(dst, a_hi, a_lo, b_hi, b_lo, start, stop):
                pe.matmul(dst, a_hi, b_hi, start=start, stop=False, skip_group_check=True)
                pe.matmul(dst, a_hi, b_lo, start=False, stop=False, skip_group_check=True)
                return pe.matmul(dst, a_lo, b_hi, start=False, stop=stop, skip_group_check=True)

            def half_chunk(c, h, dst, src_hi, src_lo, i=None, ready=None, moving=False):
                u = 2 * c + h
                pe.wait_ge(lo_ready, at(u + 1, 8, i))
                whi, wlo = unit(w_hi, u), unit(w_lo, u)
                for k in range(4 * h, 4 * h + 4):
                    if ready is not None:
                        ready(k)
                    for t in range(2):
                        o = dst[:, t * T:(t + 1) * T]
                        first, last = k == 0 and t == 0, k == KT - 1
                        if moving:
                            w = slice((k % 4) * CW, (k % 4 + 1) * CW)
                            tok = slice(t * P, (t + 1) * P)
                            ins = products(o, src_hi[:, k, tok], src_lo[:, k, tok], whi[:, w], wlo[:, w], first, last)
                        else:
                            w = slice((k % 4) * CW + t * P, (k % 4) * CW + (t + 1) * P)
                            ins = products(o, whi[:, w], wlo[:, w], src_hi[:, k, :], src_lo[:, k, :], first, last)
                ins.then_inc(unit_done, 1)

            def chunk(c, dst, src_hi, src_lo, i=None, ready=None):
                for h in range(2):
                    half_chunk(c, h, dst, src_hi, src_lo, i, ready)

            def output_chunk(c0, n, h, k_hi, k_lo, ready=None):
                u = 2 * (c0 + n) + h
                pe.wait_ge(lo_ready, u + 1)
                for r in range(2):
                    k = 4 * (n // 2) + 2 * h + r
                    if ready is not None:
                        ready(k)
                    for o in range(4):
                        w = slice(r * 2 * CW + o * P, r * 2 * CW + (o + 1) * P)
                        dst = bank[2 * (n % 2) + o // 2][:, (o % 2) * T:(o % 2 + 1) * T]
                        ins = products(dst, unit(w_hi, u)[:, w], unit(w_lo, u)[:, w], k_hi(k), k_lo(k),
                                       k == 0 and o % 2 == 0, k == KT - 1)
                ins.then_inc(unit_done, 1)

            def operand(n):
                return lambda k: pe.wait_ge(h_lo, 4 * n + k // 2 + 1) if k % 2 == 0 else None

            def square_sums(n):
                for j in range(4):
                    pe.wait_ge(sq_ready, 4 * n + j + 1)
                    for k in (2 * j, 2 * j + 1):
                        ins = pe.matmul(bank[SUM_BANK[n]][:, 0:T], ones[:], scr[:, k, :], start=k == 0, stop=k == KT - 1)
                ins.then_inc(ss_ready, 1)

            def gated_layer(c0, pair0, straight, norm_no):
                def step(c, pair, p, i, ready=None):
                    if pair > 1 or i is not None:
                        pe.wait_ge(prod_ready, at(pair - 1, 2, i))
                    chunk(c, bank[2 * (p % 2)], act_hi, act_lo, i, ready)
                    chunk(c + 1, bank[2 * (p % 2) + 1], act_hi, act_lo, i)
                for p in range(straight):
                    step(c0 + 2 * p, pair0 + p, p, None, operand(norm_no) if p == 0 else None)
                with pe.Fori(0, (PAIRS - straight) // 2) as i:
                    for j in range(2):
                        p = straight + j
                        step(c0 + 2 * p, pair0 + p, p, i)

            def down_layer(c0, pair0):
                def rows(d, i=None):
                    pe.wait_ge(hid_lo_r, at(pair0 + d + 1, 4, i))
                    for h in range(2):
                        u = 2 * (c0 + d) + h
                        pe.wait_ge(lo_ready, at(u + 1, 8, i))
                        kt = 2 * d + h
                        for o in range(KT):
                            w = slice(o * P, (o + 1) * P)
                            ins = products(bank[4 + o // 2][:, (o % 2) * T:(o % 2 + 1) * T], unit(w_hi, u)[:, w],
                                           unit(w_lo, u)[:, w], hid_hi[:, cols(kt, 8, i, 1), :], hid_lo[:, cols(kt, 8, i, 1), :],
                                           kt == 0 and o % 2 == 0, False)
                        ins.then_inc(unit_done, 1)
                for d in range(3):
                    rows(d)
                with pe.Fori(0, 2) as i:
                    for j in range(4):
                        rows(3 + j, i)

            def mod_sums(piece):
                l, first, last = PIECES[piece]
                pe.wait_ge(ada_used, ADA * l + 8 * (last // 16 + 1))
                if piece:
                    pe.wait_ge(mod_done, piece)
                for m in range(first, last + 1):
                    ins = pe.matmul(bank[7][:, m:m + 1], ada_acc[:, m // 16, m % 16 * P:(m % 16 + 1) * P], ones[:, 0:1],
                                    start=True, stop=True)
                ins.then_inc(ada_red, 1)

            pe.wait_ge(consts, 8)
            pe.wait_ge(v_landed, 16 * len(vectors))
            for n in range(4):
                pe.transpose(bank[V_BANKS[n]][:, 0:ROWS[n]], v_in[0:ROWS[n], n, :], ident[0:ROWS[n], 0:ROWS[n]]
                             ).then_inc(v_turned, 1)
            pe.wait_ge(x_landed, 32)
            for j in range(4):
                for n in range(4):
                    k, t = 2 * j + n // 2, n % 2
                    ins = pe.transpose(bank[X_BANKS[j]][:, n * P:(n + 1) * P], x_in[:, t, k * P:(k + 1) * P], ident[:])
                ins.then_inc(x_turned, 1)
            square_sums(0)

            def forget_logits():
                pe.wait_ge(wf_ready, 2)
                pe.wait_ge(f_landed, 32)
                for t in range(2):
                    o = bank[2][:, 8 * t:8 * t + 8]
                    tok = slice(t * P, (t + 1) * P)
                    for k in range(KT):
                        products(o, act_hi[:, k, tok], act_lo[:, k, tok], wf_hi[:, k, :], wf_lo[:, k, :],
                                 t == 0 and k == 0, False)
                    ins = pe.matmul(o, ones[:], fbias[:], start=False, stop=True, skip_group_check=True)
                ins.then_inc(f_done, 1)

            def forget_sums():
                pe.wait_ge(nlf_ready, 1)
                pe.wait_ge(consts, 13)
                pe.matmul(bank[2][:, 16:24], upto[:, 0:P], nlf[:, 0, :], start=True, stop=True, skip_group_check=True)
                pe.matmul(bank[2][:, 24:32], ones[:], nlf[:, 0, :], start=False, stop=False, skip_group_check=True)
                pe.matmul(bank[2][:, 24:32], upto[:, 0:P], nlf[:, 1, :], start=False, stop=True,
                          skip_group_check=True).then_inc(cum_done, 1)

            def fox_scores(h):
                s = bank[2 + h % 2]
                if h >= 2:
                    pe.wait_ge(shift_ready, h - 1)
                minus_f = [nlf[:, n, h:h + 1].broadcast_to([P, P]) for n in range(2)]
                kk = k_fox[:, h // 2, :]
                mm = lambda *a, **k: pe.matmul(*a, **k, skip_group_check=True)
                mm(s[:, 0:P], q_pad[:, h, 0:P], kk[:, 0:P], start=True, stop=False)
                mm(s[:, 0:P], minus_f[0], upto[:, 0:P], start=False, stop=True)
                mm(s[:, P:3 * P], q_pad[:, h, P:T], kk, start=False, stop=False)
                mm(s[:, P:3 * P], minus_f[0], upto[:], start=False, stop=False)
                mm(s[:, 2 * P:3 * P], minus_f[1], upto[:, 0:P], start=False, stop=True).then_inc(score_done, 1)

            def fox_turn(h):
                pe.wait_ge(p_ready, h + 1)
                if h >= 2:
                    pe.wait_ge(pt_ready, h - 1)
                for n in range(3):
                    ins = pe.transpose(bank[4 + h % 2][:, n * P:(n + 1) * P], prob[:, h % 2, n * P:(n + 1) * P], ident[:])
                ins.then_inc(turn_done, 1)

            def stick_scores(h):
                z = bank[2 + h % 2]
                if h < 2:
                    pe.wait_ge(shift_ready, 7 + h)
                else:
                    pe.wait_ge(lb_ready, h - 1)
                if h >= 4:
                    pe.wait_ge(ot1_lo, min(h - 3, 2))
                q = q_sb[:, h // 2, :]
                pe.matmul(z[:, 0:T], k_pad[:, h, 0:P], q, start=True, stop=True)
                pe.matmul(z[:, T:3 * P], k_pad[:, h, P:T], q[:, P:T], start=True, stop=True).then_inc(score_done, 1)

            def stick_sums(h):
                a = bank[4 + h % 2]
                m = sb_m[:, h % 2, :]
                pe.wait_ge(t_ready, h + 1)
                if h < 2:
                    pe.wait_ge(pt_ready, 7 + h)
                else:
                    pe.wait_ge(w_ready, h - 1)
                pe.matmul(a[:, 0:T], later[:], m[:, 0:T], start=True, stop=False, skip_group_check=True)
                pe.matmul(a[:, P:T], minus[:], m[:, T:3 * P], start=False, stop=True, skip_group_check=True)
                pe.matmul(a[:, T:3 * P], later[:], m[:, T:3 * P], start=False, stop=True,
                          skip_group_check=True).then_inc(turn_done, 1)

            def weighted_values(h):
                pe.wait_ge(pt_ready, h + 1)
                if h == 8:
                    pe.wait_ge(o_fox, 1)
                d = slice(64 * (h % 8), 64 * (h % 8) + 64)
                v = [v_tok[:, n, 64 * h:64 * h + 64] for n in range(2)]
                p = prob_t[:, h % 2, :] if h < 8 else sb_b[:, h % 2, :]
                pe.matmul(bank[6][:, d], p[:, 0:P], v[0], start=True, stop=True)
                pe.matmul(bank[7][:, d], p[:, P:T], v[0], start=True, stop=False)
                pe.matmul(bank[7][:, d], p[:, T:3 * P], v[1], start=False, stop=True).then_inc(pv_done, 1)

            def attend(s):
                if s == 0:
                    pe.wait_ge(cum_ready, 1)
                if s < 16 and s % 4 == 0:
                    pe.wait_ge(proj_free, 3 * (s // 4) + 2)
                if s < 8:
                    fox_scores(s)
                elif s < 16:
                    stick_scores(s - 8)
                if 1 <= s <= 8:
                    fox_turn(s - 1)
                elif 9 <= s <= 16:
                    stick_sums(s - 9)
                if s >= 2:
                    if s % 4 == 2:
                        pe.wait_ge(proj_free, 3 * (s // 4) + 3)
                    weighted_values(s - 2)

            def output_turn(g):
                for j in (2 * g, 2 * g + 1):
                    if g == 0:
                        pe.wait_ge(lb_ready, 3 + j)
                    else:
                        pe.wait_ge(w_ready, 5 + j)
                    for n in range(4):
                        k, t = 2 * j + n // 2, n % 2
                        pe.wait_ge(on_ready, 2 * g + t + 1)
                        ins = pe.transpose(bank[2 + j][:, n * P:(n + 1) * P], o_tok[:, t, k * P:(k + 1) * P], ident[:])
                    ins.then_inc(ot_turned, 1)

            def out1_chunk(n, h):
                if (n, h) == (0, 0):
                    pe.wait_ge(proj_free, 12)
                if (n, h) == (1, 0):
                    pe.wait_ge(lb_ready, 8)
                output_chunk(OUT1, n, h, lambda k: (fox_hi if k < 4 else act_hi)[:, k, :],
                             lambda k: (fox_lo if k < 4 else act_lo)[:, k, :],
                             lambda k: pe.wait_ge(ot1_lo, k // 2 + 1))

            for c in range(14):
                if 2 <= c < 12:
                    pe.wait_ge(proj_free, c - 1)
                for h in range(2):
                    if c < 12:
                        half_chunk(c, h, bank[c % 2], act_hi, act_lo, ready=operand(0) if c == 0 else None,
                                   moving=order1[c][0][1] == "v")
                    else:
                        out1_chunk(c - 12, h)
                    if (c, h) == (0, 0):
                        forget_logits()
                    if (c, h) == (1, 0):
                        forget_sums()
                    for s in after(STEPS1, c, h):
                        attend(s)
                    if (c, h) == (9, 1):
                        output_turn(0)
            output_turn(1)
            for n in (2, 3):
                for h in range(2):
                    out1_chunk(n, h)
            square_sums(1)
            mod_sums(0)
            gated_layer(UP1, 0, 1, 1)
            down_layer(DOWN1, 0)
            square_sums(2)
            mod_sums(1)
            square_sums(3)
            mod_sums(2)

            def head_sums(n):
                pe.wait_ge(qk_sq, n + 1)
                if n:
                    pe.wait_ge(qk_a, n)
                else:
                    pe.wait_ge(mod_done, 3)
                if n % 2 == 0:
                    ins = pe.matmul(bank[7][:], ones[:], h_sq[:], start=True, stop=True)
                else:
                    for m in range(4):
                        ins = pe.matmul(bank[7][:, m:m + 1], h_sq[:, m * P:(m + 1) * P], ones[:, 0:1], start=True, stop=True)
                ins.then_inc(qk_ss, 1)

            def attend2(s):
                if s < 8:
                    b = bank[2 + s % 2]
                    pe.wait_ge(qk_norm, 2 * (s // 2) + 2)
                    if s >= 2:
                        pe.wait_ge(m2_ready, s - 1)
                    pe.matmul(b[:, 0:P], q2[:, s, 0:P], k2[:, s, 0:P], start=True, stop=True)
                    pe.matmul(b[:, P:3 * P], q2[:, s, P:T], k2[:, s, :], start=True, stop=True).then_inc(s2_done, 1)
                if 1 <= s <= 8:
                    h = s - 1
                    pe.wait_ge(p2_ready, h + 1)
                    if h:
                        pe.wait_ge(pt2_ready, h)
                    for n in range(3):
                        ins = pe.transpose(bank[4][:, n * P:(n + 1) * P], prob2[:, h % 2, n * P:(n + 1) * P], ident[:])
                    ins.then_inc(t2_done, 1)
                if s >= 2:
                    h = s - 2
                    pe.wait_ge(pt2_ready, h + 1)
                    if h >= 2:
                        pe.wait_ge(o2_lo, h - 1)
                    if h % 2 == 0:
                        pe.wait_ge(v2_ready, h // 2 + 1)
                    o = bank[5 + h % 2]
                    v = [v2[:, n, P * h:P * h + P] for n in range(2)]
                    pt = prob2_t[:, h % 2, :]
                    pe.matmul(o[:, 0:T], v[0], pt[:, 0:T], start=True, stop=False, skip_group_check=True)
                    pe.matmul(o[:, P:T], v[1], pt[:, T:3 * P], start=False, stop=True,
                              skip_group_check=True).then_inc(pv2_done, 1)

            def out2_chunk(n, h):
                if (n, h) == (0, 0):
                    pe.wait_ge(v2_ready, 4)
                if (n, h) == (1, 0):
                    pe.wait_ge(m2_ready, 8)
                output_chunk(OUT2, n, h, lambda k: ot_hi[:, k, :], lambda k: ot_lo[:, k, :],
                             lambda k: pe.wait_ge(o2_lo, k + 1))

            for c in range(16):
                if 2 <= c < 12:
                    if c - 2 in QK_AT:
                        pe.wait_ge(qk_sq, QK_AT.index(c - 2) + 1)
                    else:
                        pe.wait_ge(v2_ready, V_AT.index(c - 2) + 1)
                for h in range(2):
                    if c < 12:
                        half_chunk(QKV + c, h, bank[c % 2], act_hi, act_lo, ready=operand(2) if c == 0 else None,
                                   moving=c in V_AT)
                    else:
                        out2_chunk(c - 12, h)
                    if h == 0 and c - 1 in QK_AT:
                        head_sums(QK_AT.index(c - 1))
                    for s in after(STEPS2, c, h):
                        attend2(s)
            square_sums(4)
            mod_sums(3)
            gated_layer(UP2, PAIRS, 3, 3)
            down_layer(DOWN2, PAIRS)
            square_sums(5)
            mod_sums(4)

            for c in range(12):
                if c >= 2:
                    pe.wait_ge(proj_free, 12 + c - 1)
                chunk(IN3 + c, bank[c % 2], act_hi, act_lo, ready=operand(4) if c == 0 else None)
            pe.wait_ge(proj_free, 24)
            for n in range(4):
                for h in range(2):
                    output_chunk(OUT3, n, h, lambda k: ot_hi[:, k, :], lambda k: ot_lo[:, k, :],
                                 lambda k: pe.wait_ge(sc_lo, k // 2 + 1) if k % 2 == 0 else None)
            mod_sums(5)
            square_sums(6)
            mod_sums(6)
            gated_layer(UP3, 2 * PAIRS, 1, 5)
            down_layer(DOWN3, 2 * PAIRS)
            for t in range(2):
                for g in range(2):
                    for n in range(4):
                        k = 4 * g + n
                        if n % 2 == 0:
                            pe.wait_ge(res_ready, 4 * 7 + k // 2 + 1)
                        ins = pe.transpose(bank[2 * t + g][:, n * P:(n + 1) * P], res[:, k, t * P:(t + 1) * P], ident[:])
                    ins.then_inc(out_turned, 1)


INPUTS = ["x", "attn_norm_g", "w_in", "forget_bias", "fox_out_g", "sb_out_g", "w_out", "ffn_norm_g", "w_up", "conv_w",
          "conv_b", "w_down", "final_norm_g", "c_2", "w_ada_2", "b_ada_2", "norm_mix_2", "norm_ffn_2", "w_qkv_2",
          "w_o_2", "q_gain_2", "k_gain_2", "w_in_2", "conv_w_2", "w_out_2", "w_gate_up_2", "w_down_2"]


def kernel(**inputs):
    import numpy as np
    import concourse.bacc as bacc
    from concourse.bass_utils import run_bass_kernel_spmd

    nc = bacc.Bacc("TRN2", target_bir_lowering=False, num_devices=1)
    arrays, args = {}, []
    for name in INPUTS:
        a = np.ascontiguousarray(inputs[name])
        arrays[f"in_{name}"] = a
        args.append(nc.dram_tensor(f"in_{name}", a.shape, mybir.dt.from_np(a.dtype), kind="ExternalInput").ap())
    args.append(nc.dram_tensor("out", (1, T, D), F32, kind="ExternalOutput").ap())
    model_kernel(nc, *args)
    return run_bass_kernel_spmd(nc, [arrays], core_ids=[0]).results[0]["out"]
```
